# Optimizing a Trainium2 kernel written in Bass

```python
import math
import jax
import jax.numpy as jnp
from jax import lax
import numpy as np

D_MODEL = 1024
BATCH = 1
SEQ = 2048
DEPTH = 1
DEC_BATCH = 1
DEC_SEQ = 64
PAST_LEN = 128

CHUNK = 64
ATTN_HEADS = 4
ATTN_HEAD_DIM = D_MODEL // 16
D_ATTN_QK = ATTN_HEADS * 2 * ATTN_HEAD_DIM
D_ATTN = ATTN_HEADS * 2 * ATTN_HEAD_DIM
REC_HEADS = 4
REC_KEY_DIM = D_MODEL // 8
REC_VAL_DIM = D_MODEL // 8
D_REC_K = REC_HEADS * REC_KEY_DIM
D_REC = REC_HEADS * REC_VAL_DIM
D_MIX = D_ATTN + D_REC
SPLIT_SIZES = (D_ATTN_QK, D_ATTN_QK, D_ATTN, D_ATTN, D_REC_K, D_REC_K, D_REC, D_REC)
PROJ_WIDTH = 2 * D_ATTN_QK + 2 * D_ATTN + 2 * D_REC_K + 2 * D_REC
Q_BLOCK = 128
EPS = 1e-6
ATTN_SCALE = ATTN_HEAD_DIM ** -0.5

kernel_name = 'hybrid_diffattn_hgrn2_streaming'

def _rmsnorm(x, g):
    xf = x.astype(jnp.float32)
    y = xf * lax.rsqrt(jnp.mean(xf * xf, axis=-1, keepdims=True) + EPS)
    return (y * g.astype(jnp.float32)).astype(x.dtype)

def _project(xn, w):
    u = xn @ w
    parts, start = [], 0
    for size in SPLIT_SIZES:
        parts.append(u[..., start:start + size])
        start += size
    return parts

def _attn_heads(qa, ka, va):
    b, s = qa.shape[:2]
    q = qa.reshape(b, s, ATTN_HEADS, 2, ATTN_HEAD_DIM)
    k = ka.reshape(b, s, ATTN_HEADS, 2, ATTN_HEAD_DIM)
    v = va.reshape(b, s, ATTN_HEADS, 2 * ATTN_HEAD_DIM)
    return q, k, v

def _diff_attend(q, k, v, q_pos, k_pos, lam, slopes):
    scores = jnp.einsum('bqhmd,bkhmd->bhmqk', q, k).astype(jnp.float32) * ATTN_SCALE
    dist = jnp.abs(q_pos[:, None] - k_pos[None, :]).astype(jnp.float32)
    bias = -slopes[:, None, None, None] * dist
    visible = (k_pos[None, :] // CHUNK) <= (q_pos[:, None] // CHUNK)
    scores = jnp.where(visible, scores + bias, -jnp.inf)
    p = jax.nn.softmax(scores, axis=-1)
    a = p[:, :, 0] - lam * p[:, :, 1]
    return jnp.einsum('bhqk,bkhe->bqhe', a.astype(v.dtype), v)

def _diff_attn_blocked(q, k, v, lam, slopes):
    b, s = q.shape[:2]
    nblk = s // Q_BLOCK
    qb = jnp.moveaxis(q.reshape(b, nblk, Q_BLOCK, ATTN_HEADS, 2, ATTN_HEAD_DIM), 1, 0)
    k_pos = jnp.arange(s, dtype=jnp.int32)
    q_pos = k_pos.reshape(nblk, Q_BLOCK)

    def one_block(args):
        q_blk, qp = args
        return _diff_attend(q_blk, k, v, qp, k_pos, lam, slopes)

    out = lax.map(one_block, (qb, q_pos))
    return jnp.moveaxis(out, 0, 1).reshape(b, s, ATTN_HEADS, 2 * ATTN_HEAD_DIM)

def _rec_inputs(qr, fr, ir, lb):
    b, s = qr.shape[:2]
    f32 = jnp.float32

    def heads(t, d):
        return jnp.swapaxes(t.reshape(b, s, REC_HEADS, d), 1, 2)

    fpre = fr.astype(f32)
    log_f = jnp.logaddexp(jnp.log(lb), jnp.log1p(-lb) + jax.nn.log_sigmoid(fpre))
    key = (1.0 - lb) * jax.nn.sigmoid(-fpre)
    q = jax.nn.silu(qr.astype(f32))
    return heads(q, REC_KEY_DIM), heads(key, REC_KEY_DIM), heads(log_f, REC_KEY_DIM), heads(ir.astype(f32), REC_VAL_DIM)

def _rec_chunk(state, q, k, log_f, v):
    c = q.shape[2]
    cum = jnp.cumsum(log_f, axis=2)
    causal = jnp.tril(jnp.ones((c, c), dtype=bool))
    diff = cum[:, :, :, None, :] - cum[:, :, None, :, :]
    decay = jnp.exp(jnp.where(causal[None, None, :, :, None], diff, -jnp.inf))
    scores = jnp.einsum('bhtsd,bhsd->bhts', decay * q[:, :, :, None, :], k)
    o = jnp.einsum('bhts,bhsv->bhtv', scores, v) + jnp.einsum('bhtd,bhdv->bhtv', q * jnp.exp(cum), state)
    last = cum[:, :, -1:, :]
    new_state = jnp.exp(last[:, :, 0, :, None]) * state + jnp.einsum('bhsd,bhsv->bhdv', k * jnp.exp(last - cum), v)
    return new_state, o

def _rec_scan(q, k, log_f, v):
    b, h, s, _ = q.shape
    nc = s // CHUNK

    def chunks(t):
        return jnp.moveaxis(t.reshape(b, h, nc, CHUNK, t.shape[-1]), 2, 0)

    s0 = jnp.zeros((b, h, REC_KEY_DIM, REC_VAL_DIM), jnp.float32)

    def step(state, inp):
        return _rec_chunk(state, *inp)

    s_fin, o = lax.scan(step, s0, (chunks(q), chunks(k), chunks(log_f), chunks(v)))
    return s_fin, jnp.moveaxis(o, 0, 2).reshape(b, h, s, REC_VAL_DIM)

def _merge(oa, orec, za, zr, sub_g, rec_g, lam_init, w_out_l):
    b, s = za.shape[:2]
    oa = _rmsnorm(oa, sub_g) * (1.0 - lam_init)
    orec = _rmsnorm(jnp.swapaxes(orec, 1, 2), rec_g)
    mix = jnp.concatenate([
        oa.reshape(b, s, D_ATTN) * jax.nn.silu(za),
        orec.reshape(b, s, D_REC).astype(za.dtype) * jax.nn.silu(zr)], axis=-1)
    return mix @ w_out_l

def setup_inputs(seed: int = 0) -> dict:
    key = jax.random.key(seed)
    ks = jax.random.split(key, 13)
    nrm = jax.random.normal
    f32 = jnp.float32
    return {
        'x_prompt': nrm(ks[0], (BATCH, SEQ, D_MODEL), f32),
        'x_sample': nrm(ks[1], (DEC_BATCH, DEC_SEQ, D_MODEL), f32),
        'cache_k': nrm(ks[2], (DEPTH, DEC_BATCH, PAST_LEN, ATTN_HEADS, 2 * ATTN_HEAD_DIM), f32),
        'cache_v': nrm(ks[3], (DEPTH, DEC_BATCH, PAST_LEN, ATTN_HEADS, 2 * ATTN_HEAD_DIM), f32),
        'state_h': 0.5 * nrm(ks[4], (DEPTH, DEC_BATCH, REC_HEADS, REC_KEY_DIM, REC_VAL_DIM), f32),
        'norm_g': 1.0 + 0.02 * nrm(ks[5], (DEPTH, D_MODEL), f32),
        'w_in': nrm(ks[6], (DEPTH, D_MODEL, PROJ_WIDTH), f32) * D_MODEL ** -0.5,
        'lambda_qk': 0.1 * nrm(ks[7], (DEPTH, 4, ATTN_HEAD_DIM), f32),
        'subln_g': 1.0 + 0.02 * nrm(ks[8], (DEPTH, 2 * ATTN_HEAD_DIM), f32),
        'rec_lb': 0.1 * nrm(ks[9], (DEPTH + 1, D_REC_K), f32),
        'rec_norm_g': 1.0 + 0.02 * nrm(ks[10], (DEPTH, REC_VAL_DIM), f32),
        'w_out': nrm(ks[11], (DEPTH, D_MIX, D_MODEL), f32) * D_MIX ** -0.5,
        'final_g': 1.0 + 0.02 * nrm(ks[12], (D_MODEL,), f32),
    }

def reference(x_prompt, x_sample, cache_k, cache_v, state_h, norm_g, w_in, lambda_qk, subln_g, rec_lb, rec_norm_g, w_out, final_g):
    f32 = jnp.float32
    slopes = jnp.exp2(-8.0 * jnp.arange(1, ATTN_HEADS + 1, dtype=f32) / ATTN_HEADS)
    lb_all = jnp.cumsum(jax.nn.softmax(rec_lb.astype(f32), axis=0), axis=0)
    bp, sp = x_prompt.shape[:2]
    bs, ts = x_sample.shape[:2]
    past = cache_k.shape[2]
    hp, hs = x_prompt, x_sample
    kp_l, vp_l, sp_l, ks_l, vs_l, ss_l = [], [], [], [], [], []
    for l in range(DEPTH):
        lam_init = 0.8 - 0.6 * math.exp(-0.3 * l)
        lq = lambda_qk[l].astype(f32)
        lam = jnp.exp(jnp.sum(lq[0] * lq[1])) - jnp.exp(jnp.sum(lq[2] * lq[3])) + lam_init
        lb = lb_all[l]

        qa, ka, va, za, qr, fr, ir, zr = _project(_rmsnorm(hp, norm_g[l]), w_in[l])
        q, k, v = _attn_heads(qa, ka, va)
        oa = _diff_attn_blocked(q, k, v, lam, slopes)
        rq, rk, rlf, rv = _rec_inputs(qr, fr, ir, lb)
        h_p, orec = _rec_scan(rq, rk, rlf, rv)
        hp = hp + _merge(oa, orec, za, zr, subln_g[l], rec_norm_g[l], lam_init, w_out[l])
        kp_l.append(k.reshape(bp, sp, ATTN_HEADS, 2 * ATTN_HEAD_DIM))
        vp_l.append(v)
        sp_l.append(h_p)

        qa, ka, va, za, qr, fr, ir, zr = _project(_rmsnorm(hs, norm_g[l]), w_in[l])
        q, k, v = _attn_heads(qa, ka, va)
        k_all = jnp.concatenate([cache_k[l].reshape(bs, past, ATTN_HEADS, 2, ATTN_HEAD_DIM).astype(k.dtype), k], axis=1)
        v_all = jnp.concatenate([cache_v[l].astype(v.dtype), v], axis=1)
        q_pos = past + jnp.arange(ts, dtype=jnp.int32)
        k_pos = jnp.arange(past + ts, dtype=jnp.int32)
        oa = _diff_attend(q, k_all, v_all, q_pos, k_pos, lam, slopes)
        rq, rk, rlf, rv = _rec_inputs(qr, fr, ir, lb)
        h_s, orec = _rec_chunk(state_h[l].astype(f32), rq, rk, rlf, rv)
        hs = hs + _merge(oa, orec, za, zr, subln_g[l], rec_norm_g[l], lam_init, w_out[l])
        ks_l.append(k.reshape(bs, ts, ATTN_HEADS, 2 * ATTN_HEAD_DIM))
        vs_l.append(v)
        ss_l.append(h_s)

    y_prompt = _rmsnorm(hp, final_g)
    y_sample = _rmsnorm(hs, final_g)
    new_k_prompt = jnp.stack(kp_l, axis=0)
    new_v_prompt = jnp.stack(vp_l, axis=0)
    new_h_prompt = jnp.stack(sp_l, axis=0)
    new_k_sample = jnp.stack(ks_l, axis=0)
    new_v_sample = jnp.stack(vs_l, axis=0)
    new_h_sample = jnp.stack(ss_l, axis=0)
    return (y_prompt, y_sample, new_k_prompt, new_v_prompt, new_h_prompt, new_k_sample, new_v_sample, new_h_sample)


_drawn_inputs = setup_inputs


def setup_inputs(seed=0):
    import zlib

    import numpy as np

    out = dict(_drawn_inputs(seed))
    spreads = {}
    factors = {}
    for name, (base, spread) in spreads.items():
        noise = np.random.default_rng([zlib.crc32(name.encode()), seed]).standard_normal(out[name].shape)
        drawn = base * np.exp(spread * noise) if base else spread * noise
        out[name] = jnp.asarray(drawn.astype(out[name].dtype))
    for name, factor in factors.items():
        out[name] = (out[name] * factor).astype(out[name].dtype)
    return out
```

```python
from contextlib import ExitStack

import numpy as np

import concourse.bass as bass
from concourse import mybir

P = 128
D_MODEL = 1024
SEQ = 2048
DEC = 64
PAST = 128
HEADS = 4
HD = 64
VD = 128
CHUNK = 64
KT = D_MODEL // P
PT = SEQ // P
NT = PT + 1
SAMPLE = NT - 1
SLOTS = NT + 1
CACHE_SLOT = PT
HALVES = (64, 32, 16, 8, 4)
BASE = 4
NS = 2 + len(HALVES)
NX = NS + 2
EPS = 1e-6
SCALE = HD ** -0.5
LAM_INIT = 0.2
MASKED = -1e30
FMAX = float(2.0 ** 59)


def slot_of(t):
    return t if t < PT else CACHE_SLOT + 1


def keys_of(t):
    if t < PT:
        return 0, P * (t + 1)
    return CACHE_SLOT * P, PAST + DEC


def chunks_of(t):
    k0, n = keys_of(t)
    return [(k0 + c, min(512, n - c), c) for c in range(0, n, 512)]


def blocks_of(t, c):
    k0, w, _ = chunks_of(t)[c]
    return [(b, (k0 + b) // P, min(P, w - b)) for b in range(0, w, P)]


NCH = sum(len(chunks_of(t)) for t in range(NT))
T_USES = NCH + 3 * NT
QK_USES = 2 * NCH + 2 * NT
XRING = 3
RAWRING = 4
EVEN, ODD = (NT + 1) // 2, NT // 2
PAIRS = PT // 2


def build(nc, x_prompt, x_sample, cache_k, cache_v, state_h, norm_g, w_in, lambda_qk, subln_g, rec_lb,
          rec_norm_g, w_out, final_g, y_prompt, y_sample, new_k_prompt, new_v_prompt, new_h_prompt,
          new_k_sample, new_v_sample, new_h_sample):
    f32, f32r, i32 = mybir.dt.float32, mybir.dt.float32r, mybir.dt.int32
    ALU, ACT, AX = mybir.AluOpType, mybir.ActivationFunctionType, mybir.AxisListType
    ctx = ExitStack()
    with ctx:
        def sb(name, shape, dt=f32):
            return ctx.enter_context(nc.sbuf_tensor(name, shape, dt))

        def ps(name):
            return ctx.enter_context(nc.psum_tensor(name, [P, 2, 512], f32))

        sems = {}

        def sem(name):
            sems[name] = ctx.enter_context(nc.semaphore(name))
            return sems[name]

        xs = nc.dram_tensor("xs", [NT, P, 2 * KT * P], f32).ap()
        mix = nc.dram_tensor("mix", [NT, P, 2, HEADS, VD], f32).ap()

        w_hi = sb("w_hi", [P, KT, 1024], f32r)
        w_lo = sb("w_lo", [P, KT, 1024], f32r)
        w_raw = sb("w_raw", [P, RAWRING, 1024])
        xr = sb("xr", [P, XRING, 2, KT, P], f32r)
        kp = sb("kp", [P, 2, SLOTS * P], f32r)
        vv = sb("vv", [P, SLOTS, VD])
        scores = sb("scores", [P, 2, SEQ])
        bias = sb("bias", [P, SEQ])
        at = sb("at", [P, 2, 512])
        qn = sb("qn", [P, 8, P], f32r)
        q2 = sb("q2", [P, 2, 2, P], f32r)
        kn = sb("kn", [P, 2, P])
        ez = sb("ez", [P, P])
        gzr = sb("gzr", [P, P])
        gz = sb("gz", [P, 2, P])
        fb = sb("fb", [P, 4, P])
        rc = sb("rc", [P, 3, P])
        nb = sb("nb", [P, 3, P])
        gr = sb("gr", [P, 2, P])
        vr = sb("vr", [P, 2, P])
        lf = sb("lf", [P, P])
        qt = sb("qt", [P, P])
        kt_ = sb("kt_", [P, P])
        dd = sb("dd", [P, NX, P])
        xx = sb("xx", [P, NX, P])
        kq = sb("kq", [P, 2, NS, P])
        kl, ql = kq[:, 0], kq[:, 1]
        masked = sb("masked", [P, NS - 1, P])
        causal = sb("causal", [P, NS - 1, P])
        st = sb("st", [P, P])
        kd = sb("kd", [P, P])
        state = sb("state", [P, P])
        state_s = sb("state_s", [P, P])
        mx = sb("mx", [P, 2, 2, P])
        junk = sb("junk", [P, 2 * P])
        junk_rows = (at[:, :, :].rearrange("p a c -> p (a c)"),
                     dd[:, 0:8, :].rearrange("p a c -> p (a c)"))
        gains = kq[:, :, :, :].rearrange("p a n c -> p (a n c)")[:, 0:D_MODEL]
        xn = vv[:, 0:2 * KT, :].rearrange("p (a k) c -> p a (k c)", a=2)
        kc = sb("kc", [P, P])
        ident = sb("ident", [P, P])
        ones = sb("ones", [P, P])
        subg = sb("subg", [P, P])
        recg = sb("recg", [P, P])
        lamv = masked[:, 0:2, :].rearrange("p a (b d) -> p (a b) d", b=2)
        lbr = sb("lbr", [P, 2, HEADS])
        lbw = sb("lbw", [P, 4, HEADS])
        lb = sb("lb", [P, HEADS])
        oml = sb("oml", [P, HEADS])
        lbh = sb("lbh", [P, 2])
        lam = sb("lam", [P, 6])
        half = sb("half", [P, 2])
        ssq = sb("ssq", [P, 2])
        ms = sb("ms", [P, 2])
        rs = sb("rs", [P, 2])
        tsq = sb("tsq", [P, 2])
        tms = sb("tms", [P, 2])
        trs = sb("trs", [P, 2])
        rsa = sb("rsa", [P, 1])
        mxs = sb("mxs", [P, 2, 4])
        nmx = sb("nmx", [P, 2])
        sums = sb("sums", [P, 2])
        rsum = sb("rsum", [P, 2])
        cneg = sb("cneg", [P, 1])

        pab = ps("pab")
        qkb = ps("qkb")
        tb = ps("tb")
        oar = ps("oar")

        PER = dict(
            w_hi_ready=KT, w_lo_ready=KT, w_freed=KT - 1, proj_done=NT, a_evac=NT, b_evac=NT, qk_split=NT,
            pa_free=NT, nat_b=NT, pb_free=NT, gate_a=NT, gate_r=NT, rect_t=NT, q_t=NT, k_t=NT,
            t_evac=T_USES, qk_done=2 * NCH, kscore_done=NT, qk_free=QK_USES, neg_max=NT, prob_ready=NT,
            combined=NT, at_t=NCH, pv_done=NT, cum_ready=NT, dist_ready=NT, decay_ready=NT, lev_ready=NT,
            kd_t=NT, kd_evac=NT, rec_acc=NT, rec_out=NT, sumsq=NT, rs_ready=NT, fin_done=NT, head_set=1,
            cache_split=1, vec_chain=6 * NT + 1, pool_chain=2 * NT,
            k_out0=16 * EVEN, k_out1=16 * ODD, v_out=16 * NT, mix_out0=16 * EVEN, mix_out1=16 * ODD, h_out=32,
            cache_in=48)
        PRIME = dict(pa_free=1, pb_free=1, fin_done=1, qk_free=2, t_evac=2, gate_a=1, gate_r=1,
                     k_out0=16, k_out1=16, v_out=16, mix_out0=16, mix_out1=16, h_out=16,
                     pro_xn=2, pro_t=2, pro_lo=2, xs_out0=16, xs_out1=16, fo_mm=2, fo_add=2, y_out0=16, y_out1=16)
        PRIMED_BY = dict(gpsimd=("gate_a", "gate_r", "k_out0", "k_out1", "v_out", "mix_out0", "mix_out1", "h_out",
                                 "xs_out0", "xs_out1", "y_out0", "y_out1"),
                         vector=("pa_free", "pb_free", "fin_done", "qk_free", "pro_xn", "pro_lo", "fo_add"),
                         scalar=("t_evac",), tensor=("pro_t", "fo_mm"))
        assert sorted(PRIME) == sorted(sum(PRIMED_BY.values(), ()))

        S = {name: ctx.enter_context(nc.semaphore(name)) for name in list(PER) + [
            "x_in0", "x_in1", "gains_in", "const_in", "raw_in0", "raw_in1", "raw_in2", "raw_in3", "xs_out0",
            "xs_out1", "xr_in0", "xr_in1", "xr_in2", "y_out0", "y_out1", "mixin0", "mixin1",
            "pro_sq", "pro_rs", "pro_xn", "pro_t", "pro_hi", "pro_lo", "pro_rs_mean", "fo_rs_mean", "masks_ready", "table_ready",
            "lam_dots", "lb_shifted", "setup_exp", "vec_setup", "pool_setup",
            "apart", "fo_t", "fo_hi", "fo_lo", "fo_mm", "fo_add", "fo_sq", "fo_rs", "fo_y"]}

        def need(eng, h, name, n):
            eng.wait_ge(S[name], h * PER[name] + (PRIME.get(name, 0) + n))

        def apart(eng):
            eng.sem_inc(S["apart"], 1)

        def past(eng, name, n):
            eng.wait_ge(S[name], n + PRIME.get(name, 0))

        def prime(engine, who):
            for name in PRIMED_BY[who]:
                engine.sem_inc(S[name], PRIME[name])

        block = ctx.enter_context(nc.Block())

        t_use, qk_use, qk_index, at_index = {}, {}, {}, {}
        for t in range(NT + 1):
            if t > 0:
                for part in range(2):
                    qk_use["rec", t - 1, part] = len(qk_use)
                for c in range(len(chunks_of(t - 1))):
                    t_use["at", t - 1, c] = len(t_use)
                    at_index[t - 1, c] = len(at_index)
            if t < NT:
                for what in ("rec", "q", "k"):
                    t_use[what, t] = len(t_use)
                for c in range(len(chunks_of(t))):
                    for m in range(2):
                        qk_use["qk", t, c, m] = len(qk_use)
                        qk_index[t, c, m] = len(qk_index)
        assert len(t_use) == T_USES and len(qk_use) == QK_USES and T_USES % 2 == 0 and QK_USES % 2 == 0

        XR_PER = [len(range(s, NT, XRING)) for s in range(XRING)]
        x_rows = x_prompt[0].rearrange("(t p) d -> t p d", p=P)
        y_rows = y_prompt[0].rearrange("(t p) d -> t p d", p=P)

        def flat(ap):
            return ap.rearrange("o p d -> (o p) d")

        @block.sync
        def _(sp):
            def pro_load(i, par):
                sp.dma_start(scores[:, par, 0:1024], flat(x_rows[bass.ds(2 * i + par, 1)])
                             ).then_inc(S[f"x_in{par}"], 16)

            def pro_store(i, par):
                past(sp, "pro_lo", 2 * i + (par + 1))
                apart(sp)
                sp.dma_start(flat(xs[bass.ds(2 * i + par, 1)]), xr[:, par].rearrange("p a k c -> p (a k c)").bitcast(f32)
                             ).then_inc(S[f"xs_out{par}"], 16)

            def raw_load(weights, kt):
                slot = kt % RAWRING
                if weights is None:
                    sp.dma_start(w_raw[:, slot, :], w_out[0, kt * P:(kt + 1) * P, :]
                                 ).then_inc(S[f"raw_in{slot}"], 16)
                else:
                    rows = w_in[0, kt * P:(kt + 1) * P, :].rearrange("p (g h c) -> p g h c", g=8, h=HEADS)
                    sp.dma_start(w_raw[:, slot, :].rearrange("p (g c) -> p g c", g=8),
                                 rows[:, :, bass.ds(weights, 1), :].rearrange("p g o c -> p g (o c)")
                                 ).then_inc(S[f"raw_in{slot}"], 16)

            def x_load(t):
                slot = t % XRING
                sp.dma_start(xr[:, slot].rearrange("p a k c -> p (a k c)").bitcast(f32), xs[t]
                             ).then_inc(S[f"xr_in{slot}"], 16)

            pro_load(0, 0)
            sp.dma_start(gains[:, :], norm_g[0:1, :].to_broadcast([P, D_MODEL])).then_inc(S["gains_in"], 16)
            pro_load(0, 1)
            with nc.allow_non_contiguous_dma(reason="small constants"):
                sp.dma_start(lamv[:, :, :].rearrange("p a d -> p (a d)"),
                             lambda_qk.rearrange("l a d -> l (a d)").to_broadcast([P, 4 * HD])
                             ).then_inc(S["const_in"], 16)
                sp.dma_start(subg[:, :], subln_g[0:1, :].to_broadcast([P, VD])).then_inc(S["const_in"], 16)
                sp.dma_start(recg[:, :], rec_norm_g[0:1, :].to_broadcast([P, VD])).then_inc(S["const_in"], 16)
                for r in range(2):
                    sp.dma_start(lbr[:, r, :], rec_lb[r].rearrange("(h d) -> d h", h=HEADS)
                                 ).then_inc(S["const_in"], 16)
            for kt in range(RAWRING):
                raw_load(0, kt)
            with sp.Fori(0, PAIRS - 1) as i:
                for par in range(2):
                    past(sp, "pro_xn", 2 * i + (par + 1))
                    apart(sp)
                    pro_load(i + 1, par)
                    pro_store(i, par)
            past(sp, "pro_xn", PT - 1)
            apart(sp)
            sp.dma_start(scores[0:DEC, 0, 0:1024], x_sample[0]).then_inc(S["x_in0"], 16)
            for par in range(2):
                pro_store(PAIRS - 1, par)
            pro_store(PAIRS, 0)
            past(sp, "xs_out0", 16 * EVEN)
            apart(sp)
            past(sp, "xs_out1", 16 * ODD)
            apart(sp)
            for t in range(XRING):
                x_load(t)
            for kt in range(RAWRING, KT):
                sp.wait_ge(S["w_lo_ready"], kt - RAWRING + 1)
                raw_load(0, kt)

            def mix_store(h, t):
                need(sp, h, "fin_done", t + 1)
                apart(sp)
                sp.dma_start(mix[t, :, :, bass.ds(h, 1), :].rearrange("p b o c -> p b (o c)"),
                             mx[:, t % 2, :, :]).then_inc(S[f"mix_out{t % 2}"], 16)
                if t == PT - 1:
                    sp.dma_start(new_h_prompt[0, 0, bass.ds(h, 1)].rearrange("o d v -> (o d) v"), state[:, :]
                                 ).then_inc(S["h_out"], 16)

            def head(h, last):
                def one_head(ap):
                    return ap[:, bass.ds(h, 1), :].rearrange("t o d -> t (o d)")

                following = None if last else h + 1
                for t in range(NT):
                    if 1 <= t and t + 2 < NT:
                        need(sp, h, "proj_done", t)
                        apart(sp)
                        x_load(t + 2)
                    if t == 1:
                        sp.dma_start(kc[:, :], one_head(cache_k[0, 0])).then_inc(S["cache_in"], 16)
                        sp.dma_start(vv[:, CACHE_SLOT, :], one_head(cache_v[0, 0])).then_inc(S["cache_in"], 16)
                        sp.dma_start(state_s[:, :], state_h[0, 0, bass.ds(h, 1)].rearrange("o d v -> (o d) v")
                                     ).then_inc(S["cache_in"], 16)
                    if t == 2:
                        for kt in range(RAWRING):
                            need(sp, h, "w_lo_ready", RAWRING + kt + 1)
                            apart(sp)
                            raw_load(following, kt)
                    need(sp, h, "a_evac", t + 1)
                    apart(sp)
                    ko, vo = (new_k_prompt, new_v_prompt) if t < PT else (new_k_sample, new_v_sample)
                    r0, n = (t * P, P) if t < PT else (0, DEC)
                    sp.dma_start(one_head(ko[0, 0, r0:r0 + n]), kn[0:n, t % 2, :]).then_inc(S[f"k_out{t % 2}"], 16)
                    sp.dma_start(one_head(vo[0, 0, r0:r0 + n]), vv[0:n, slot_of(t), :]).then_inc(S["v_out"], 16)
                    if t > 0:
                        mix_store(h, t - 1)
                if not last:
                    need(sp, h, "proj_done", NT)
                    apart(sp)
                    for t in range(XRING):
                        x_load(t)
                for kt in range(RAWRING, KT):
                    need(sp, h, "w_lo_ready", KT + kt - RAWRING + 1)
                    apart(sp)
                    raw_load(following, kt)
                mix_store(h, SAMPLE)
                sp.dma_start(new_h_sample[0, 0, bass.ds(h, 1)].rearrange("o d v -> (o d) v"), state_s[:, :]
                             ).then_inc(S["h_out"], 16)
                need(sp, h, "h_out", 32)
                apart(sp)
                need(sp, h, "v_out", 16 * NT)
                apart(sp)

            with sp.Fori(0, HEADS - 1) as h:
                head(h, False)
            head(HEADS - 1, True)

            need(sp, HEADS - 1, "mix_out0", 16 * EVEN)
            apart(sp)
            need(sp, HEADS - 1, "mix_out1", 16 * ODD)
            apart(sp)
            sp.dma_start(gains[:, :], final_g.rearrange("(o d) -> o d", o=1).to_broadcast([P, D_MODEL])
                         ).then_inc(S["gains_in"], 16)

            def epi_load(i, par):
                cols = slice(1024 * par, 1024 * par + 1024)
                sp.dma_start(scores[:, 0, cols],
                             mix[bass.ds(2 * i + par, 1)].rearrange("o p b h c -> (o p) (b h c)")
                             ).then_inc(S[f"mixin{par}"], 16)
                sp.dma_start(scores[:, 1, cols], flat(x_rows[bass.ds(2 * i + par, 1)])
                             ).then_inc(S[f"mixin{par}"], 16)

            def epi_store(i, par):
                sp.wait_ge(S["fo_y"], 2 * i + (par + 1))
                apart(sp)
                sp.dma_start(flat(y_rows[bass.ds(2 * i + par, 1)]), xn[:, par, :]).then_inc(S[f"y_out{par}"], 16)

            for par in range(2):
                epi_load(0, par)
            with sp.Fori(0, PAIRS - 1) as i:
                for par in range(2):
                    epi_store(i, par)
                    epi_load(i + 1, par)
            epi_store(PAIRS - 1, 0)
            sp.dma_start(scores[:, 0, 0:1024], mix[SAMPLE].rearrange("p b h c -> p (b h c)")
                         ).then_inc(S["mixin0"], 16)
            sp.dma_start(scores[0:DEC, 1, 0:1024], x_sample[0]).then_inc(S["mixin0"], 16)
            epi_store(PAIRS - 1, 1)
            sp.wait_ge(S["fo_y"], NT)
            sp.dma_start(y_sample[0], xn[0:DEC, 0, :]).then_inc(S["y_out0"], 16)
            past(sp, "y_out0", 16 * EVEN)
            apart(sp)
            past(sp, "y_out1", 16 * ODD)
            apart(sp)
            need(sp, HEADS - 1, "k_out0", 16 * EVEN)
            apart(sp)
            need(sp, HEADS - 1, "k_out1", 16 * ODD)
            apart(sp)

        @block.tensor
        def _(pe):
            mm, tr = nc.tensor.matmul, nc.tensor.transpose
            pe.wait_ge(S["masks_ready"], 1)

            prime(pe, "tensor")

            def pro_tile(i, par):
                past(pe, "pro_xn", 2 * i + (par + 1))
                past(pe, "pro_lo", 2 * i + (par - 1))
                bank = (tb, qkb)[par]
                for kt in range(KT):
                    last = tr(bank[:, kt // 4, P * (kt % 4):P * (kt % 4) + P], xn[:, par, P * kt:P * kt + P],
                              ident[:, :])
                last.then_inc(S["pro_t"], 1)

            with pe.Fori(0, PAIRS) as i:
                for par in range(2):
                    pro_tile(i, par)
            pro_tile(PAIRS, 0)
            past(pe, "pro_lo", NT)

            def project(h, t):
                slot = t % XRING
                pe.wait_ge(S[f"xr_in{slot}"], h * (16 * XR_PER[slot]) + 16 * (t // XRING + 1))
                need(pe, h, "pa_free", t)
                need(pe, h, "pb_free", t)
                for kt in range(KT):
                    if t == 0:
                        need(pe, h, "w_hi_ready", kt + 1)
                        need(pe, h, "w_lo_ready", kt + 1)
                    if kt == 6 and t > 0:
                        rec_scores(h, t - 1)
                    for part in range(2):
                        x = xr[:, slot, part, kt, :]
                        for w in ((w_hi, w_lo) if part == 0 else (w_hi,)):
                            for b in range(2):
                                end = kt == KT - 1 and part == 1
                                last = mm(pab[:, b, :], x, w[:, kt, 512 * b:512 * b + 512],
                                          start=(kt == 0 and part == 0 and w is w_hi), stop=end)
                    if t == SAMPLE and kt < KT - 1:
                        last.then_inc(S["w_freed"], 1)
                last.then_inc(S["proj_done"], 1)

            def rec_scores(h, t):
                n = P if t < PT else DEC
                need(pe, h, "lev_ready", t + 1)
                for part, blocks in enumerate((range(1, 5), range(5, NS))):
                    u = qk_use["rec", t, part]
                    need(pe, h, "qk_free", u - 1)
                    for j, b in enumerate(blocks):
                        q = NS - 2 if b == 1 else b - 2
                        last = mm(qkb[:, u % 2, P * j:P * j + P], kl[:, b, :], ql[:, q, :], start=True, stop=True)
                last.then_inc(S["kscore_done"], 1)
                need(pe, h, "fin_done", t)
                apart(pe)
                tr(oar[0:n, 1, 256:384], kl[:, 0, 0:n], ident[:, :]).then_inc(S["kd_t"], 1)

            def rec_output(h, t):
                n = P if t < PT else DEC
                need(pe, h, "kd_evac", t + 1)
                need(pe, h, "rec_acc", t + 1)
                if t == 0:
                    need(pe, h, "head_set", 1)
                if t == SAMPLE:
                    need(pe, h, "cache_in", 48)
                s_in = state if t < PT else state_s
                mm(oar[:, 1, 0:P], st[:, :], vr[:, t % 2, :], start=True, stop=False)
                mm(oar[:, 1, 0:P], ql[:, NS - 1, :], s_in[:, :], start=False, stop=True)
                mm(oar[:, 1, P:2 * P], kd[0:n, :], vr[0:n, t % 2, :], start=True, stop=True
                   ).then_inc(S["rec_out"], 1)

            def attend(h, t):
                need(pe, h, "combined", t + 1)
                if t == SAMPLE:
                    need(pe, h, "cache_in", 48)
                need(pe, h, "fin_done", t)
                chunks = chunks_of(t)

                def transposes(c):
                    u = t_use["at", t, c]
                    need(pe, h, "t_evac", u - 1)
                    apart(pe)
                    for b, _, n in blocks_of(t, c):
                        last = tr(tb[0:n, u % 2, b:b + P], scores[:, 0, chunks[c][2] + b:chunks[c][2] + b + n],
                                  ident[:, :])
                    last.then_inc(S["at_t"], 1)

                def values(c):
                    u = t_use["at", t, c]
                    need(pe, h, "t_evac", u + 1)
                    blocks = blocks_of(t, c)
                    for j, (b, slot, n) in enumerate(blocks):
                        last = mm(oar[:, 0, 0:VD], at[0:n, u % 2, b:b + P], vv[0:n, slot, :],
                                  start=(c == 0 and j == 0), stop=(c == len(chunks) - 1 and j == len(blocks) - 1))
                    return last

                transposes(0)
                for c in range(len(chunks)):
                    if c + 1 < len(chunks):
                        transposes(c + 1)
                    last = values(c)
                last.then_inc(S["pv_done"], 1)

            def transpose_inputs(h, t):
                u = t_use["rec", t]
                need(pe, h, "t_evac", u - 1)
                need(pe, h, "nat_b", t + 1)
                tr(tb[:, u % 2, 0:P], nb[:, 0, :], ident[:, :])
                tr(tb[:, u % 2, P:2 * P], rc[:, 2, :], ident[:, :])
                tr(tb[:, u % 2, 2 * P:3 * P], nb[:, 2, :], ident[:, :]).then_inc(S["rect_t"], 1)
                u = t_use["q", t]
                need(pe, h, "t_evac", u - 1)
                need(pe, h, "qk_split", t + 1)
                for j in range(4):
                    last = tr(tb[:, u % 2, P * j:P * j + P], qn[:, j, :].bitcast(f32), ident[:, :])
                last.then_inc(S["q_t"], 1)
                u = t_use["k", t]
                need(pe, h, "t_evac", u - 1)
                if t == SAMPLE:
                    need(pe, h, "cache_split", 1)
                    for j in range(4):
                        last = tr(tb[:, u % 2, P * j:P * j + P], qn[:, (6, 4, 7, 5)[j], :].bitcast(f32), ident[:, :])
                else:
                    for j in range(2):
                        last = tr(tb[:, u % 2, P * j:P * j + P], qn[:, 4 + j, :].bitcast(f32), ident[:, :])
                last.then_inc(S["k_t"], 1)

            def qk(h, t):
                need(pe, h, "t_evac", t_use["k", t] + 1)
                for c, (k0, w, _) in enumerate(chunks_of(t)):
                    for m in range(2):
                        u = qk_use["qk", t, c, m]
                        need(pe, h, "qk_free", u - 1)
                        for part in range(2):
                            last = mm(qkb[:, u % 2, 0:w], q2[:, m, part, :], kp[:, m, k0:k0 + w],
                                      start=(part == 0), stop=(part == 1))
                        last.then_inc(S["qk_done"], 1)

            with pe.Fori(0, HEADS) as h:
                for t in range(NT + 1):
                    if t < NT:
                        project(h, t)
                    else:
                        rec_scores(h, t - 1)
                    if t > 0:
                        rec_output(h, t - 1)
                        attend(h, t - 1)
                    if t < NT:
                        transpose_inputs(h, t)
                        qk(h, t)

            def epi_transposes(i, par):
                pe.wait_ge(S[f"mixin{par}"], 32 * i + 32)
                if isinstance(i, int) and i == 0 and par == 0:
                    pass
                else:
                    pe.wait_ge(S["fo_lo"], 2 * i + par)
                for kt in range(KT):
                    last = tr(tb[:, kt // 4, P * (kt % 4):P * (kt % 4) + P],
                              scores[:, 0, 1024 * par + P * kt:1024 * par + P * kt + P], ident[:, :])
                last.then_inc(S["fo_t"], 1)

            def epi_project(i, par):
                pe.wait_ge(S["fo_lo"], 2 * i + (par + 1))
                past(pe, "fo_add", 2 * i + (par - 1))
                bank = (pab, qkb)[par]
                for kt in range(KT):
                    for part in range(2):
                        x = xr[:, par, part, kt, :]
                        for w in ((w_hi, w_lo) if part == 0 else (w_hi,)):
                            for b in range(2):
                                last = mm(bank[:, b, :], x, w[:, kt, 512 * b:512 * b + 512],
                                          start=(kt == 0 and part == 0 and w is w_hi),
                                          stop=(kt == KT - 1 and part == 1))
                last.then_inc(S["fo_mm"], 1)

            need(pe, HEADS - 1, "fin_done", NT)
            need(pe, HEADS - 1, "t_evac", T_USES)
            need(pe, HEADS - 1, "qk_free", QK_USES)
            need(pe, HEADS, "w_hi_ready", KT)
            need(pe, HEADS, "w_lo_ready", KT)
            epi_transposes(0, 0)
            with pe.Fori(0, PAIRS) as i:
                epi_transposes(i, 1)
                epi_project(i, 0)
                epi_transposes(i + 1, 0)
                epi_project(i, 1)
            epi_project(PAIRS, 0)

        @block.scalar
        def _(act):
            F = nc.scalar.activation
            prime(act, "scalar")

            def pro_square(i, par):
                act.wait_ge(S[f"x_in{par}"], 16 * i + 16)
                F(junk_rows[par], scores[:, par, 0:1024], ACT.Square, accum_out=tsq[:, par:par + 1]
                  ).then_inc(S["pro_sq"], 1)

            def pro_hi(i, par):
                act.wait_ge(S["pro_t"], 2 * i + (par + 1 + PRIME["pro_t"]))
                past(act, f"xs_out{par}", 16 * i)
                F(xr[:, par, 0], (tb, qkb)[par][:, :, :], ACT.Copy).then_inc(S["pro_hi"], 1)

            act.wait_ge(S["lam_dots"], 2)
            F(lam[:, 2:4], lam[:, 0:2], ACT.Exp).then_inc(S["setup_exp"], 1)
            act.wait_ge(S["lb_shifted"], 2)
            F(lbw[:, 2:4, :], lbw[:, 0:2, :], ACT.Exp).then_inc(S["setup_exp"], 1)
            pro_square(0, 0)
            with act.Fori(0, PAIRS) as i:
                pro_square(i, 1)
                pro_hi(i, 0)
                pro_square(i + 1, 0)
                pro_hi(i, 1)
            pro_hi(PAIRS, 0)

            def split_weights(h):
                for kt in range(KT):
                    if not (isinstance(h, int) and h < 0):
                        if kt < KT - 1:
                            need(act, h, "w_freed", kt + 1)
                        else:
                            need(act, h, "proj_done", NT)
                    act.wait_ge(S[f"raw_in{kt % RAWRING}"], (h + 1) * 32 + (16 * (kt // RAWRING) + 16))
                    F(w_hi[:, kt, :], w_raw[:, kt % RAWRING, :], ACT.Copy).then_inc(S["w_hi_ready"], 1)

            split_weights(-1)

            def copy_decayed_keys(h, t):
                n = P if t < PT else DEC
                need(act, h, "kd_t", t + 1)
                F(kd[0:n, :], oar[0:n, 1, 256:384], ACT.Copy).then_inc(S["kd_evac"], 1)

            def attention_columns(h, t):
                need(act, h, "proj_done", t + 1)
                pa = pab[:, 0, :]
                q_out = qn[:, 0:4, :].rearrange("p (m a) (d e) -> p m a d e", m=2, d=2)[:, :, 0]
                q_in = pa[:, 0:P].rearrange("p (m e) -> p m e", m=2).unsqueeze(2).to_broadcast([P, 2, 2, HD])
                F(q_out, q_in, ACT.Copy)
                F(qn[:, 4:6, 0:HD], pa[:, P:2 * P].rearrange("p (m e) -> p m e", m=2), ACT.Copy)
                need(act, h, f"k_out{t % 2}", 16 * (t // 2))
                F(kn[:, t % 2, :], pa[:, P:2 * P], ACT.Copy)
                if t == 0:
                    need(act, h, "v_out", 0)
                F(vv[:, slot_of(t), :], pa[:, 2 * P:3 * P], ACT.Copy)
                F(ez[:, :], pa[:, 3 * P:4 * P], ACT.Exp, scale=-1.0).then_inc(S["a_evac"], 1)

            def recurrence_columns(h, t):
                F(fb[:, :, :], pab[:, 1, :].rearrange("p (g c) -> p g c", g=4), ACT.Exp, scale=-1.0)
                F(vr[:, t % 2, :], pab[:, 1, 2 * P:3 * P], ACT.Copy).then_inc(S["b_evac"], 1)

            def copy_weights(h, t):
                for c in range(len(chunks_of(t))):
                    u = t_use["at", t, c]
                    w = P * len(blocks_of(t, c))
                    need(act, h, "at_t", at_index[t, c] + 1)
                    F(at[:, u % 2, 0:w], tb[:, u % 2, 0:w], ACT.Copy).then_inc(S["t_evac"], 1)

            def sum_squares(h, t):
                need(act, h, "rec_out", t + 1)
                need(act, h, "pv_done", t + 1)
                F(junk[:, 0:P], oar[:, 0, 0:P], ACT.Square, scale=rsum[:, 0:1], accum_out=ssq[:, 0:1])
                F(junk[:, P:2 * P], oar[:, 1, 0:P], ACT.Square, accum_out=ssq[:, 1:2]).then_inc(S["sumsq"], 1)

            def copy_transposed(h, t):
                u = t_use["rec", t]
                need(act, h, "rect_t", t + 1)
                F(lf[:, :], tb[:, u % 2, P:2 * P], ACT.Ln, scale=lbh[:, 1:2], bias=lbh[:, 0:1])
                F(qt[:, :], tb[:, u % 2, 0:P], ACT.Copy)
                F(kt_[:, :], tb[:, u % 2, 2 * P:3 * P], ACT.Copy, scale=lbh[:, 1:2]).then_inc(S["t_evac"], 1)
                u = t_use["q", t]
                need(act, h, "q_t", t + 1)
                F(q2[:, :, :, :].rearrange("p m a c -> p (m a c)"), tb[:, u % 2, :], ACT.Copy
                  ).then_inc(S["t_evac"], 1)
                u = t_use["k", t]
                need(act, h, "k_t", t + 1)
                first, w = (slot_of(t) * P, P) if t < PT else (CACHE_SLOT * P, 2 * P)
                F(kp[:, :, first:first + w], tb[:, u % 2, 0:2 * w].rearrange("p (m c) -> p m c", m=2), ACT.Copy
                  ).then_inc(S["t_evac"], 1)

            def softmax_exp(h, t):
                n = keys_of(t)[1]
                need(act, h, "neg_max", t + 1)
                for m in range(2):
                    last = F(scores[:, m, 0:n], scores[:, m, 0:n], ACT.Exp, bias=nmx[:, m:m + 1], scale=SCALE,
                             accum_out=sums[:, m:m + 1])
                last.then_inc(S["prob_ready"], 1)

            def decay_exp(h, t):
                need(act, h, "dist_ready", t + 1)
                F(xx[:, :, :], dd[:, :, :], ACT.Exp).then_inc(S["decay_ready"], 1)

            with act.Fori(0, HEADS) as h:
                for t in range(NT + 1):
                    if t > 0:
                        copy_decayed_keys(h, t - 1)
                    if t < NT:
                        attention_columns(h, t)
                        recurrence_columns(h, t)
                    if t > 0:
                        copy_weights(h, t - 1)
                        sum_squares(h, t - 1)
                    if t < NT:
                        if t == 0:
                            need(act, h, "head_set", 1)
                        copy_transposed(h, t)
                        softmax_exp(h, t)
                        decay_exp(h, t)
                    if t == SAMPLE:
                        split_weights(h)

            def epi_hi(i, par):
                act.wait_ge(S["fo_t"], 2 * i + (par + 1))
                past(act, "fo_mm", 2 * i + (par - 1))
                F(xr[:, par, 0], tb[:, :, :], ACT.Copy).then_inc(S["fo_hi"], 1)

            def epi_square(i, par):
                past(act, "fo_add", 2 * i + (par + 1))
                F(junk_rows[par], scores[:, 1, 1024 * par:1024 * par + 1024], ACT.Square,
                  accum_out=tsq[:, par:par + 1]).then_inc(S["fo_sq"], 1)

            epi_hi(0, 0)
            with act.Fori(0, PAIRS) as i:
                epi_hi(i, 1)
                epi_square(i, 0)
                epi_hi(i + 1, 0)
                epi_square(i, 1)
            epi_square(PAIRS, 0)

        @block.vector
        def _(dve):
            v = nc.vector
            tt, stt, ts = v.tensor_tensor, v.scalar_tensor_tensor, v.tensor_scalar
            prime(dve, "vector")
            setup = [0]

            def setup_link(ins):
                setup[0] += 1
                ins.then_inc(S["vec_setup"], 1)
                dve.wait_ge(S["vec_setup"], setup[0])

            v.memset(ones[:, :], 1.0)
            dve.wait_ge(S["const_in"], 80)
            for j in range(2):
                v.tensor_tensor_reduce(out=ez[:, HD * j:HD * j + HD], in0=lamv[:, 2 * j, :], in1=lamv[:, 2 * j + 1, :], scale=1.0,
                                       scalar=0.0, op0=ALU.mult, op1=ALU.add, accum_out=lam[:, j:j + 1]
                                       ).then_inc(S["lam_dots"], 1)
            setup_link(tt(lb[:, :], lbr[:, 0, :], lbr[:, 1, :], ALU.max))
            for r in range(2):
                tt(lbw[:, r, :], lbr[:, r, :], lb[:, :], ALU.subtract).then_inc(S["lb_shifted"], 1)
            dve.wait_ge(S["setup_exp"], 2)
            setup_link(tt(lam[:, 4:5], lam[:, 3:4], lam[:, 2:3], ALU.subtract))
            setup_link(v.tensor_scalar_add(lam[:, 5:6], lam[:, 4:5], -LAM_INIT))
            setup_link(tt(lb[:, :], lbw[:, 2, :], lbw[:, 3, :], ALU.add))
            setup_link(v.reciprocal(oml[:, :], lb[:, :]))
            setup_link(tt(lb[:, :], lbw[:, 2, :], oml[:, :], ALU.mult))
            setup_link(tt(oml[:, :], lbw[:, 3, :], oml[:, :], ALU.mult))
            setup_link(ts(subg[:, :], subg[:, :], 1.0 - LAM_INIT, None, ALU.mult))
            dve.wait_ge(S["table_ready"], 2)
            setup_link(stt(bias[:, :], bias[:, :], -1.0, bias[:, :], ALU.mult, ALU.min))
            v.memset(bias[0:CHUNK, SEQ - CHUNK:SEQ], MASKED).then_inc(S["vec_setup"], 1)

            def pro_normalise(i, par):
                dve.wait_ge(S["pro_rs"], 2 * i + (par + 1))
                past(dve, "pro_t", 2 * i + (par - 1))
                stt(xn[:, par, :], scores[:, par, 0:1024], trs[:, par:par + 1], gains[:, :], ALU.mult, ALU.mult
                    ).then_inc(S["pro_xn"], 1)

            def pro_lo(i, par):
                dve.wait_ge(S["pro_hi"], 2 * i + (par + 1))
                tt(xr[:, par, 1].rearrange("p k c -> p (k c)"),
                   (tb, qkb)[par][:, :, :].rearrange("p b c -> p (b c)"),
                   xr[:, par, 0].rearrange("p k c -> p (k c)").bitcast(f32), ALU.subtract
                   ).then_inc(S["pro_lo"], 1)

            dve.wait_ge(S["gains_in"], 16)
            pro_normalise(0, 0)
            with dve.Fori(0, PAIRS) as i:
                pro_normalise(i, 1)
                pro_lo(i, 0)
                pro_normalise(i + 1, 0)
                pro_lo(i, 1)
            pro_lo(PAIRS, 0)

            def split_weights(h):
                for kt in range(KT):
                    need(dve, h + 1, "w_hi_ready", kt + 1)
                    tt(w_lo[:, kt, :], w_raw[:, kt % RAWRING, :], w_hi[:, kt, :].bitcast(f32), ALU.subtract
                       ).then_inc(S["w_lo_ready"], 1)

            split_weights(-1)

            chain = [0]

            def link(h, ins):
                chain[0] += 1
                ins.then_inc(S["vec_chain"], 1)
                need(dve, h, "vec_chain", chain[0])

            def head_start(h):
                need(dve, h, "h_out", 0)
                v.memset(state[:, :], 0.0)
                v.tensor_copy(lbh[:, 0:1], lb[:, bass.ds(h, 1)])
                v.tensor_copy(lbh[:, 1:2], oml[:, bass.ds(h, 1)]).then_inc(S["head_set"], 1)

            def sum_scores(h, t):
                need(dve, h, "kscore_done", t + 1)
                for part, (a, b) in enumerate(((0, 4), (4, NS - 1))):
                    u = qk_use["rec", t, part]
                    tt(masked[:, a:b, :], qkb[:, u % 2, 0:P * (b - a)].rearrange("p (l c) -> p l c", c=P),
                       causal[:, a:b, :], ALU.mult).then_inc(S["qk_free"], 1)
                need(dve, h, "qk_free", u + 1)
                v.tensor_reduce(st[:, :], masked[:, :, :].rearrange("p l c -> p c l"), AX.X, ALU.add
                                ).then_inc(S["rec_acc"], 1)

            def attention_columns(h, t):
                need(dve, h, "a_evac", t + 1)
                pa = pab[:, 0, :]
                q_blocks = qn[:, 0:4, :].rearrange("p (m a) (d e) -> p m a d e", m=2, d=2)
                q_in = pa[:, 0:P].rearrange("p (m e) -> p m e", m=2).unsqueeze(2).to_broadcast([P, 2, 2, HD])
                tt(q_blocks[:, :, 1], q_in, q_blocks[:, :, 0].bitcast(f32), ALU.subtract)
                tt(qn[:, 4:6, HD:P], pa[:, P:2 * P].rearrange("p (m e) -> p m e", m=2),
                   qn[:, 4:6, 0:HD].bitcast(f32), ALU.subtract).then_inc(S["qk_split"], 1)
                if t == SAMPLE:
                    need(dve, h, "cache_in", 48)
                    k_in = kc[:, :].rearrange("p (m e) -> p m e", m=2)
                    link(h, v.tensor_copy(qn[:, 6:8, 0:HD], k_in))
                    tt(qn[:, 6:8, HD:P], k_in, qn[:, 6:8, 0:HD].bitcast(f32), ALU.subtract
                       ).then_inc(S["cache_split"], 1)
                link(h, v.tensor_scalar_add(ez[:, :], ez[:, :], 1.0))
                link(h, v.reciprocal(ez[:, :], ez[:, :]))
                need(dve, h, "gate_a", t)
                tt(gzr[:, :], pa[:, 3 * P:4 * P], ez[:, :], ALU.mult).then_inc(S["pa_free"], 1)

            def recurrence_columns(h, t):
                need(dve, h, "b_evac", t + 1)
                ts(rc[:, 2, :], fb[:, 1, :], FMAX, 1.0, ALU.min, ALU.add)
                link(h, v.tensor_scalar_add(rc[:, 0:2, :], fb[:, 0:4:3, :], 1.0))
                link(h, v.reciprocal(rc[:, :, :], rc[:, :, :]))
                need(dve, h, "gate_r", t)
                tt(nb[:, 0:2, :], pab[:, 1, :].rearrange("p (g c) -> p g c", g=4)[:, 0:4:3, :], rc[:, 0:2, :],
                   ALU.mult).then_inc(S["pb_free"], 1)
                stt(nb[:, 2, :], fb[:, 1, :], FMAX, rc[:, 2, :], ALU.min, ALU.mult).then_inc(S["nat_b"], 1)

            def finish(h, t):
                need(dve, h, "rs_ready", t + 1)
                need(dve, h, "gate_r", t + 1)
                need(dve, h, f"mix_out{t % 2}", 16 * (t // 2))
                stt(mx[:, t % 2, 0, :], oar[:, 0, 0:P], rsa[:, 0:1], gz[:, t % 2, :], ALU.mult, ALU.mult)
                s, at_last = (state, P - 1) if t < PT else (state_s, DEC - 1)
                stt(s[:, :], s[:, :], xx[:, NX - 1, at_last:at_last + 1], oar[:, 1, P:2 * P], ALU.mult, ALU.add)
                stt(mx[:, t % 2, 1, :], oar[:, 1, 0:P], rs[:, 1:2], gr[:, t % 2, :], ALU.mult, ALU.mult
                    ).then_inc(S["fin_done"], 1)

            def accumulate_decay(h, t):
                need(dve, h, "t_evac", t_use["rec", t] + 1)
                v.tensor_tensor_scan(dd[:, NX - 1, :], ones[:, :], lf[:, :], 0.0, ALU.mult, ALU.add
                                     ).then_inc(S["cum_ready"], 1)

            def biased_scores(h, t):
                chunks = chunks_of(t)
                zero = SEQ - P - P * (t if t < PT else 1)
                for c, (_, w, off) in enumerate(chunks):
                    for m in range(2):
                        u = qk_use["qk", t, c, m]
                        need(dve, h, "qk_done", qk_index[t, c, m] + 1)
                        if c > 0:
                            need(dve, h, "qk_free", u - 1)
                        apart(dve)
                        v.tensor_tensor_reduce(
                            out=scores[:, m, off:off + w], in0=qkb[:, u % 2, 0:w],
                            in1=bias[:, zero + off:zero + off + w], scale=1.0,
                            scalar=(mxs[:, m, c - 1:c] if c else -3e38), op0=ALU.add, op1=ALU.max,
                            accum_out=mxs[:, m, c:c + 1]).then_inc(S["qk_free"], 1)
                need(dve, h, "qk_free", u + 1)
                ts(nmx[:, :], mxs[:, :, len(chunks) - 1], -SCALE, None, ALU.mult).then_inc(S["neg_max"], 1)

            def combine(h, t):
                n = keys_of(t)[1]
                need(dve, h, "prob_ready", t + 1)
                link(h, v.reciprocal(rsum[:, :], sums[:, :]))
                link(h, stt(cneg[:, :], sums[:, 0:1], rsum[:, 1:2], lam[:, 5:6], ALU.mult, ALU.mult))
                stt(scores[:, 0, 0:n], scores[:, 1, 0:n], cneg[:, 0:1], scores[:, 0, 0:n], ALU.mult, ALU.add
                    ).then_inc(S["combined"], 1)

            def apply_decay(h, t):
                need(dve, h, "decay_ready", t + 1)
                tt(kl[:, :, :], kt_[:, :].unsqueeze(1).to_broadcast([P, NS, P]), xx[:, 0:NS, :], ALU.mult)
                tt(ql[:, :, :], qt[:, :].unsqueeze(1).to_broadcast([P, NS, P]), xx[:, NX - NS:NX, :], ALU.mult
                   ).then_inc(S["lev_ready"], 1)

            with dve.Fori(0, HEADS) as h:
                head_start(h)
                for t in range(NT + 1):
                    if t > 0:
                        sum_scores(h, t - 1)
                    if t < NT:
                        attention_columns(h, t)
                        recurrence_columns(h, t)
                    if t > 0:
                        finish(h, t - 1)
                    if t < NT:
                        accumulate_decay(h, t)
                        biased_scores(h, t)
                        combine(h, t)
                        apply_decay(h, t)
                    if t == SAMPLE:
                        split_weights(h)
                ts(bias[:, :], bias[:, :], 0.25, None, ALU.mult)
            assert chain[0] == PER["vec_chain"], chain[0]

            def epi_lo(i, par):
                dve.wait_ge(S["fo_hi"], 2 * i + (par + 1))
                tt(xr[:, par, 1].rearrange("p k c -> p (k c)"), tb[:, :, :].rearrange("p b c -> p (b c)"),
                   xr[:, par, 0].rearrange("p k c -> p (k c)").bitcast(f32), ALU.subtract
                   ).then_inc(S["fo_lo"], 1)

            def epi_add(i, par):
                dve.wait_ge(S["fo_mm"], 2 * i + (par + 1 + PRIME["fo_mm"]))
                rows = scores[:, 1, 1024 * par:1024 * par + 1024]
                tt(rows, (pab, qkb)[par][:, :, :].rearrange("p b c -> p (b c)"), rows, ALU.add
                   ).then_inc(S["fo_add"], 1)

            def epi_normalise(i, par):
                dve.wait_ge(S["fo_rs"], 2 * i + (par + 1))
                past(dve, f"y_out{par}", 16 * i)
                stt(xn[:, par, :], scores[:, 1, 1024 * par:1024 * par + 1024], trs[:, par:par + 1], gains[:, :],
                    ALU.mult, ALU.mult).then_inc(S["fo_y"], 1)

            dve.wait_ge(S["gains_in"], 32)
            epi_lo(0, 0)
            with dve.Fori(0, PAIRS) as i:
                epi_lo(i, 1)
                epi_add(i, 0)
                epi_normalise(i, 0)
                epi_lo(i + 1, 0)
                epi_add(i, 1)
                epi_normalise(i, 1)
            epi_add(PAIRS, 0)
            epi_normalise(PAIRS, 0)

        @block.gpsimd
        def _(pool):
            g = nc.gpsimd
            prime(pool, "gpsimd")
            setup = [0]

            def setup_link(ins):
                setup[0] += 1
                ins.then_inc(S["pool_setup"], 1)
                pool.wait_ge(S["pool_setup"], setup[0])

            g.memset(half[:, :], -0.5)
            g.memset(ident[:, :], 0.0)
            setup_link(g.memset(causal[:, :, :], 1.0))
            g.affine_select(out=ident[:, :], in_=ident[:, :], compare_op=ALU.not_equal, fill=1.0, base=0,
                            pattern=[[-1, P]], channel_multiplier=1).then_inc(S["masks_ready"], 1)
            table = xx[:, 0:8, :].rearrange("p a c -> p (a c)").bitcast(i32)
            for part in range(2):
                setup_link(g.iota(table, pattern=[[-2, 1024]], base=2 * (SEQ - P - 1024 * part),
                                  channel_multiplier=2))
                g.tensor_copy(bias[:, 1024 * part:1024 * part + 1024], table).then_inc(S["table_ready"], 1)
                pool.wait_ge(S["table_ready"], part + 1)

            def row_scale(done, i, par):
                ready, signal = done
                pool.wait_ge(S[ready], 2 * i + (par + 1))
                apart(pool)
                g.tensor_scalar(tms[:, par:par + 1], tsq[:, par:par + 1], 1.0 / D_MODEL, EPS, ALU.mult, ALU.add
                                ).then_inc(S[signal + "_mean"], 1)
                pool.wait_ge(S[signal + "_mean"], 2 * i + (par + 1))
                g.tensor_tensor(trs[:, par:par + 1], tms[:, par:par + 1], half[:, 0:1], ALU.pow
                                ).then_inc(S[signal], 1)

            prologue = ("pro_sq", "pro_rs")
            with pool.Fori(0, PAIRS) as i:
                for par in range(2):
                    row_scale(prologue, i, par)
            row_scale(prologue, PAIRS, 0)

            def keep(out, pattern, base, step):
                return g.affine_select(out=out, in_=out, compare_op=ALU.is_ge, fill=0.0, base=base,
                                       pattern=pattern, channel_multiplier=step)

            for j, size in enumerate((BASE,) + tuple(2 * s for s in HALVES)):
                nblk = P // size
                out = causal[:, j, :].rearrange("p (b r) -> p b r", b=nblk)
                setup_link(keep(out, [[-size, nblk], [0, size]], 0, 1))
                if j == 0:
                    setup_link(keep(out, [[size, nblk], [1, size]], 0, -1))
                else:
                    setup_link(keep(out, [[size, nblk], [0, size]], size // 2 - 1, -1))
                    setup_link(keep(out, [[0, nblk], [1, size]], -(size // 2), 0))

            chain = [0]

            def link(h, ins):
                chain[0] += 1
                ins.then_inc(S["pool_chain"], 1)
                need(pool, h, "pool_chain", chain[0])

            def gates(h, t):
                need(pool, h, "pa_free", t + 1)
                g.tensor_tensor(gz[:, t % 2, :], gzr[:, :], subg[:, :], ALU.mult).then_inc(S["gate_a"], 1)
                need(pool, h, "nat_b", t + 1)
                g.tensor_tensor(gr[:, t % 2, :], nb[:, 1, :], recg[:, :], ALU.mult).then_inc(S["gate_r"], 1)

            def head_scales(h, t):
                need(pool, h, "sumsq", t + 1)
                apart(pool)
                link(h, g.tensor_scalar(ms[:, :], ssq[:, :], 1.0 / VD, EPS, ALU.mult, ALU.add))
                link(h, g.tensor_tensor(rs[:, :], ms[:, :], half[:, :], ALU.pow))
                g.tensor_tensor(rsa[:, :], rs[:, 0:1], rsum[:, 0:1], ALU.mult).then_inc(S["rs_ready"], 1)

            def exponents(h, t):
                n = P if t < PT else DEC
                need(pool, h, "cum_ready", t + 1)
                cum = dd[:, NX - 1, :]
                sub = ALU.subtract
                for j, s in enumerate(HALVES):
                    c = cum.rearrange("p (b a r) -> p b a r", a=2, r=s)
                    o = dd[:, 2 + j, :].rearrange("p (b a r) -> p b a r", a=2, r=s)
                    ref = c[:, :, 0, s - 1:s].to_broadcast([P, P // (2 * s), s])
                    g.tensor_tensor(o[:, :, 0, :], ref, c[:, :, 0, :], sub)
                    g.tensor_tensor(o[:, :, 1, :], c[:, :, 1, :], ref, sub)
                c = cum.rearrange("p (b r) -> p b r", r=BASE)
                ref = c[:, :, 1:2].to_broadcast([P, P // BASE, BASE])
                g.tensor_tensor(dd[:, 1, :].rearrange("p (b r) -> p b r", r=BASE), ref, c, sub)
                g.tensor_tensor(dd[:, NX - 2, :].rearrange("p (b r) -> p b r", r=BASE), c, ref, sub)
                g.tensor_tensor(dd[:, 0, 0:n], cum[:, n - 1:n].to_broadcast([P, n]), cum[:, 0:n], sub
                                ).then_inc(S["dist_ready"], 1)

            with pool.Fori(0, HEADS) as h:
                for t in range(NT + 1):
                    if t < NT:
                        gates(h, t)
                    if t > 0:
                        head_scales(h, t - 1)
                    if t < NT:
                        exponents(h, t)
            assert chain[0] == PER["pool_chain"]

            final = ("fo_sq", "fo_rs")
            with pool.Fori(0, PAIRS) as i:
                for par in range(2):
                    row_scale(final, i, par)
            row_scale(final, PAIRS, 0)


_INS = ["x_prompt", "x_sample", "cache_k", "cache_v", "state_h", "norm_g", "w_in", "lambda_qk", "subln_g", "rec_lb",
        "rec_norm_g", "w_out", "final_g"]
_OUTS = [(1, SEQ, D_MODEL), (1, DEC, D_MODEL), (1, 1, SEQ, HEADS, 2 * HD), (1, 1, SEQ, HEADS, VD),
         (1, 1, HEADS, VD, VD), (1, 1, DEC, HEADS, 2 * HD), (1, 1, DEC, HEADS, VD), (1, 1, HEADS, VD, VD)]


def kernel(**inputs):
    import concourse.bacc as bacc
    from concourse.bass_utils import run_bass_kernel_spmd

    nc = bacc.Bacc("TRN2", target_bir_lowering=False, num_devices=1)
    arrays, args = {}, []
    for name in _INS:
        a = np.ascontiguousarray(inputs[name])
        arrays[f"in_{name}"] = a
        args.append(nc.dram_tensor(f"in_{name}", a.shape, mybir.dt.from_np(a.dtype), kind="ExternalInput").ap())
    for i, shape in enumerate(_OUTS):
        args.append(nc.dram_tensor(f"out_{i}", shape, mybir.dt.float32, kind="ExternalOutput").ap())
    build(nc, *args)
    r = run_bass_kernel_spmd(nc, [arrays], core_ids=[0])
    return tuple(r.results[0][f"out_{i}"] for i in range(len(_OUTS)))
```

```python
from contextlib import ExitStack

import numpy as np

import concourse.bass as bass
from concourse import mybir

P = 128
D_MODEL = 1024
SEQ = 2048
DEC = 64
PAST = 128
HEADS = 4
HD = 64
VD = 128
CHUNK = 64
KT = D_MODEL // P
PT = SEQ // P
NT = PT + 1
SAMPLE = NT - 1
SLOTS = NT + 1
CACHE_SLOT = PT
HALVES = (64, 32, 16, 8, 4)
BASE = 4
NS = 2 + len(HALVES)
NX = NS + 2
EPS = 1e-6
SCALE = HD ** -0.5
LAM_INIT = 0.2
MASKED = -1e30
FMAX = float(2.0 ** 59)


def slot_of(t):
    return t if t < PT else CACHE_SLOT + 1


def keys_of(t):
    if t < PT:
        return 0, P * (t + 1)
    return CACHE_SLOT * P, PAST + DEC


def chunks_of(t):
    k0, n = keys_of(t)
    return [(k0 + c, min(512, n - c), c) for c in range(0, n, 512)]


def blocks_of(t, c):
    k0, w, _ = chunks_of(t)[c]
    return [(b, (k0 + b) // P, min(P, w - b)) for b in range(0, w, P)]


def exp_first(t):
    return t > 0 and (t == NT or len(chunks_of(t - 1)) <= 2)


def lo_of(kt):
    return ("w_lo_pool", LO_POOL.index(kt) + 1) if kt in LO_POOL else ("w_lo_vec", kt + 1)


NCH = sum(len(chunks_of(t)) for t in range(NT))
T_USES = NCH + 3 * NT
QK_USES = 2 * NCH + 2 * NT
XRING = 3
RAWRING = 4
LO_POOL = (5, 6, 7)
LO_PER = dict(w_lo_vec=KT - len(LO_POOL), w_lo_pool=len(LO_POOL))
EVEN, ODD = (NT + 1) // 2, NT // 2
PAIRS = PT // 2


def build(nc, x_prompt, x_sample, cache_k, cache_v, state_h, norm_g, w_in, lambda_qk, subln_g, rec_lb,
          rec_norm_g, w_out, final_g, y_prompt, y_sample, new_k_prompt, new_v_prompt, new_h_prompt,
          new_k_sample, new_v_sample, new_h_sample):
    f32, f32r, i32 = mybir.dt.float32, mybir.dt.float32r, mybir.dt.int32
    ALU, ACT, AX = mybir.AluOpType, mybir.ActivationFunctionType, mybir.AxisListType
    ctx = ExitStack()
    with ctx:
        def sb(name, shape, dt=f32):
            return ctx.enter_context(nc.sbuf_tensor(name, shape, dt))

        def ps(name):
            return ctx.enter_context(nc.psum_tensor(name, [P, 2, 512], f32))

        sems = {}

        def sem(name):
            sems[name] = ctx.enter_context(nc.semaphore(name))
            return sems[name]

        xs = nc.dram_tensor("xs", [NT, P, 2 * KT * P], f32).ap()
        mix = nc.dram_tensor("mix", [NT, P, 2, HEADS, VD], f32).ap()

        w_hi = sb("w_hi", [P, KT, 1024], f32r)
        w_lo = sb("w_lo", [P, KT, 1024], f32r)
        w_raw = sb("w_raw", [P, RAWRING, 1024])
        xr = sb("xr", [P, XRING, 2, KT, P], f32r)
        kp = sb("kp", [P, 2, SLOTS * P], f32r)
        vv = sb("vv", [P, SLOTS, VD])
        scores = sb("scores", [P, 2, SEQ])
        bias = sb("bias", [P, SEQ])
        at = sb("at", [P, 2, 512])
        qn = sb("qn", [P, 8, P], f32r)
        q2 = sb("q2", [P, 2, 2, P], f32r)
        kn = sb("kn", [P, 2, P])
        zz = sb("zz", [P, 2, P])
        ez = sb("ez", [P, 2, P])
        gate = sb("gate", [P, 2, 2, P])
        fb = sb("fb", [P, 2, P])
        rc = sb("rc", [P, 2, P])
        nb = sb("nb", [P, 2, P])
        vr = sb("vr", [P, 2, P])
        lf = sb("lf", [P, P])
        qt = sb("qt", [P, P])
        kt_ = sb("kt_", [P, P])
        dd = sb("dd", [P, NX, P])
        xx = sb("xx", [P, NX, P])
        kq = sb("kq", [P, 2, NS, P])
        kl, ql = kq[:, 0], kq[:, 1]
        masked = sb("masked", [P, NS - 1, P])
        causal = sb("causal", [P, NS - 1, P])
        st = sb("st", [P, P])
        kd = sb("kd", [P, P])
        state = sb("state", [P, P])
        state_s = sb("state_s", [P, P])
        mx = sb("mx", [P, 2, 2, P])
        junk = sb("junk", [P, 2 * P])
        junk_rows = (at[:, :, :].rearrange("p a c -> p (a c)"),
                     dd[:, 0:8, :].rearrange("p a c -> p (a c)"))
        x_raw, x_norm, x_gain = (w_raw[:, j, :] for j in range(3))
        w_raw0 = scores[:, :, :].rearrange("p m (a c) -> p (m a) c", c=1024)
        gains = kq[:, :, :, :].rearrange("p a n c -> p (a n c)")[:, 0:D_MODEL]
        xn = vv[:, 0:2 * KT, :].rearrange("p (a k) c -> p a (k c)", a=2)
        kc = sb("kc", [P, P])
        ident = sb("ident", [P, P])
        ones = sb("ones", [P, P])
        gains2 = sb("gains2", [P, 2, P])
        lamv = masked[:, 0:2, :].rearrange("p a (b d) -> p (a b) d", b=2)
        lbr = sb("lbr", [P, 2, HEADS])
        lbw = sb("lbw", [P, 4, HEADS])
        lb = sb("lb", [P, HEADS])
        oml = sb("oml", [P, HEADS])
        lbh = sb("lbh", [P, 2])
        lam = sb("lam", [P, 6])
        half = sb("half", [P, 2])
        ssq = sb("ssq", [P, 2])
        ms = sb("ms", [P, 2])
        rs = sb("rs", [P, 2])
        tsq = sb("tsq", [P, 2])
        tms = sb("tms", [P, 2])
        trs = sb("trs", [P, 2])
        rsa = sb("rsa", [P, 1])
        mxs = sb("mxs", [P, 2, 4])
        nmx = sb("nmx", [P, 2])
        sums = sb("sums", [P, 2])
        rsum = sb("rsum", [P, 2])
        cneg = sb("cneg", [P, 1])

        pab = ps("pab")
        qkb = ps("qkb")
        tb = ps("tb")
        oar = ps("oar")

        PER = dict(
            w_hi_ready=KT, w_freed=KT - 1, proj_b=NT, proj_done=NT, a_evac=NT, b_evac=NT, qk_split=NT,
            nat_b=NT, pb_free=NT, z_ready=NT, gates=NT, rect_t=NT, q_t=NT, k_t=NT,
            t_evac=T_USES, qk_done=2 * NCH, kscore_done=NT, qk_free=QK_USES, neg_max=NT, prob_ready=NT,
            combined=NT, at_t=NCH, pv_done=NT, cum_ready=NT, dist_ready=NT, decay_ready=NT, k_decayed=NT,
            q_decayed=NT, kd_t=NT, kd_evac=NT, rec_acc=NT, rec_out=NT, sumsq=NT, rs_ready=NT, fin_done=NT,
            head_set=1, cache_split=1, vec_chain=5 * NT + 1, pool_chain=3 * NT,
            k_out0=16 * EVEN, k_out1=16 * ODD, v_out=16 * NT, mix_out0=16 * EVEN, mix_out1=16 * ODD, h_out=32,
            cache_in=48, **LO_PER)
        PRIME = dict(qk_split=1, pb_free=1, fin_done=1, qk_free=2, t_evac=2, gates=1,
                     k_out0=16, k_out1=16, v_out=16, mix_out0=16, mix_out1=16, h_out=16,
                     fo_mm=2, fo_add=2, y_out0=16, y_out1=16)
        PRIMED_BY = dict(gpsimd=("gates", "k_out0", "k_out1", "v_out", "mix_out0", "mix_out1", "h_out",
                                 "y_out0", "y_out1"),
                         vector=("qk_split", "pb_free", "fin_done", "qk_free", "fo_add"),
                         scalar=("t_evac",), tensor=("fo_mm",))
        assert sorted(PRIME) == sorted(sum(PRIMED_BY.values(), ()))

        S = {name: ctx.enter_context(nc.semaphore(name)) for name in list(PER) + [
            "x_in", "gains_in", "const_in", "raw_in0", "raw_in1", "raw_in2", "raw_in3", "xs_out0",
            "xs_out1", "xs_out2", "xr_in0", "xr_in1", "xr_in2", "y_out0", "y_out1", "mixin0", "mixin1", "rowsin0", "rowsin1",
            "x_sq", "x_rs", "x_rs_mean", "x_rows", "x_t", "x_hi", "x_lo", "fo_rs_mean",
            "masks_ready", "table_ready", "lam_dots", "lb_shifted", "setup_exp", "vec_setup", "pool_setup",
            "apart", "fo_t", "fo_hi", "fo_lo", "fo_mm", "fo_add", "fo_sq", "fo_rs", "fo_y"]}

        def need(eng, h, name, n):
            eng.wait_ge(S[name], h * PER[name] + (PRIME.get(name, 0) + n))

        def apart(eng):
            eng.sem_inc(S["apart"], 1)

        def past(eng, name, n):
            eng.wait_ge(S[name], n + PRIME.get(name, 0))

        def prime(engine, who):
            for name in PRIMED_BY[who]:
                engine.sem_inc(S[name], PRIME[name])

        block = ctx.enter_context(nc.Block())

        t_use, qk_use, qk_index, at_index = {}, {}, {}, {}
        for t in range(NT + 1):
            if t > 0:
                for c in range(len(chunks_of(t - 1))):
                    for m in range(2):
                        qk_use["qk", t - 1, c, m] = len(qk_use)
                        qk_index[t - 1, c, m] = len(qk_index)
                for part in range(2):
                    qk_use["rec", t - 1, part] = len(qk_use)
            if t < NT:
                t_use["rec", t] = len(t_use)
            if t > 0:
                for c in range(len(chunks_of(t - 1))):
                    t_use["at", t - 1, c] = len(t_use)
                    at_index[t - 1, c] = len(at_index)
            if t < NT:
                for what in ("q", "k"):
                    t_use[what, t] = len(t_use)
        assert len(t_use) == T_USES and len(qk_use) == QK_USES and T_USES % 2 == 0 and QK_USES % 2 == 0

        XR_PER = [len(range(s, NT, XRING)) for s in range(XRING)]
        x_rows = x_prompt[0].rearrange("(t p) d -> t p d", p=P)
        y_rows = y_prompt[0].rearrange("(t p) d -> t p d", p=P)

        def flat(ap):
            return ap.rearrange("o p d -> (o p) d")

        @block.sync
        def _(sp):
            def raw_load(weights, kt):
                slot = kt % RAWRING
                place = w_raw0[:, slot, :] if isinstance(weights, int) and weights == 0 else w_raw[:, slot, :]
                if weights is None:
                    sp.dma_start(place, w_out[0, kt * P:(kt + 1) * P, :]).then_inc(S[f"raw_in{slot}"], 16)
                else:
                    rows = w_in[0, kt * P:(kt + 1) * P, :].rearrange("p (g h c) -> p g h c", g=8, h=HEADS)
                    sp.dma_start(place.rearrange("p (g c) -> p g c", g=8),
                                 rows[:, :, bass.ds(weights, 1), :].rearrange("p g o c -> p g (o c)")
                                 ).then_inc(S[f"raw_in{slot}"], 16)

            def rows_load(t):
                if t > 0:
                    sp.wait_ge(S["x_rows"], t)
                if t < PT:
                    sp.dma_start(x_raw, x_rows[t]).then_inc(S["x_in"], 16)
                else:
                    sp.dma_start(x_raw[0:DEC, :], x_sample[0]).then_inc(S["x_in"], 16)

            def xs_store(t):
                sp.wait_ge(S["x_lo"], t + 1)
                sp.dma_start(xs[t], xr[:, t % XRING].rearrange("p a k c -> p (a k c)").bitcast(f32)
                             ).then_inc(S[f"xs_out{t % XRING}"], 16)

            def x_load(t):
                slot = t % XRING
                sp.dma_start(xr[:, slot].rearrange("p a k c -> p (a k c)").bitcast(f32), xs[t]
                             ).then_inc(S[f"xr_in{slot}"], 16)

            rows_load(0)
            sp.dma_start(x_gain, norm_g[0:1, :].to_broadcast([P, D_MODEL])).then_inc(S["gains_in"], 16)
            for kt in range(RAWRING):
                raw_load(0, kt)
            rows_load(1)
            with nc.allow_non_contiguous_dma(reason="small constants"):
                sp.dma_start(lamv[:, :, :].rearrange("p a d -> p (a d)"),
                             lambda_qk.rearrange("l a d -> l (a d)").to_broadcast([P, 4 * HD])
                             ).then_inc(S["const_in"], 16)
                sp.dma_start(gains2[:, 0, :], subln_g[0:1, :].to_broadcast([P, VD])).then_inc(S["const_in"], 16)
                sp.dma_start(gains2[:, 1, :], rec_norm_g[0:1, :].to_broadcast([P, VD])).then_inc(S["const_in"], 16)
                for r in range(2):
                    sp.dma_start(lbr[:, r, :], rec_lb[r].rearrange("(h d) -> d h", h=HEADS)
                                 ).then_inc(S["const_in"], 16)
            for kt in range(RAWRING, KT):
                name, n = lo_of(kt - RAWRING)
                sp.wait_ge(S[name], n)
                raw_load(0, kt)

            def mix_store(h, t):
                need(sp, h, "fin_done", t + 1)
                apart(sp)
                sp.dma_start(mix[t, :, :, bass.ds(h, 1), :].rearrange("p b o c -> p b (o c)"),
                             mx[:, t % 2, :, :]).then_inc(S[f"mix_out{t % 2}"], 16)
                if t == PT - 1:
                    sp.dma_start(new_h_prompt[0, 0, bass.ds(h, 1)].rearrange("o d v -> (o d) v"), state[:, :]
                                 ).then_inc(S["h_out"], 16)

            def head(h, last):
                def one_head(ap):
                    return ap[:, bass.ds(h, 1), :].rearrange("t o d -> t (o d)")

                first = isinstance(h, int) and h == 0
                following = None if last else h + 1

                def raw_ahead(kt):
                    name, n = lo_of(RAWRING + kt)
                    need(sp, h, name, n)
                    apart(sp)
                    raw_load(following, kt)

                for t in range(NT):
                    if first:
                        if t + 2 < NT:
                            rows_load(t + 2)
                        if t < 2:
                            xs_store(t)
                        if 1 <= t < NT - 1:
                            xs_store(t + 1)
                    elif 1 <= t and t + 2 < NT:
                        need(sp, h, "proj_done", t)
                        apart(sp)
                        x_load(t + 2)
                    if t == 1:
                        if first:
                            need(sp, h, "proj_done", 1)
                        sp.dma_start(kc[:, :], one_head(cache_k[0, 0])).then_inc(S["cache_in"], 16)
                        sp.dma_start(vv[:, CACHE_SLOT, :], one_head(cache_v[0, 0])).then_inc(S["cache_in"], 16)
                        sp.dma_start(state_s[:, :], state_h[0, 0, bass.ds(h, 1)].rearrange("o d v -> (o d) v")
                                     ).then_inc(S["cache_in"], 16)
                    if t == 2:
                        if first:
                            raw_ahead(RAWRING - 1)
                        else:
                            for kt in range(RAWRING):
                                raw_ahead(kt)
                    if first and t == SAMPLE:
                        for kt in range(RAWRING - 1):
                            raw_ahead(kt)
                    need(sp, h, "a_evac", t + 1)
                    apart(sp)
                    ko, vo = (new_k_prompt, new_v_prompt) if t < PT else (new_k_sample, new_v_sample)
                    r0, n = (t * P, P) if t < PT else (0, DEC)
                    sp.dma_start(one_head(ko[0, 0, r0:r0 + n]), kn[0:n, t % 2, :]).then_inc(S[f"k_out{t % 2}"], 16)
                    sp.dma_start(one_head(vo[0, 0, r0:r0 + n]), vv[0:n, slot_of(t), :]).then_inc(S["v_out"], 16)
                    if t > 0:
                        mix_store(h, t - 1)
                if first:
                    for j in range(XRING):
                        sp.wait_ge(S[f"xs_out{j}"], 16 * XR_PER[j])
                if not last:
                    need(sp, h, "proj_done", NT)
                    apart(sp)
                    for t in range(XRING):
                        x_load(t)
                for kt in range(RAWRING, KT):
                    name, n = lo_of(kt - RAWRING)
                    need(sp, h + 1, name, n)
                    apart(sp)
                    raw_load(following, kt)
                mix_store(h, SAMPLE)
                sp.dma_start(new_h_sample[0, 0, bass.ds(h, 1)].rearrange("o d v -> (o d) v"), state_s[:, :]
                             ).then_inc(S["h_out"], 16)
                need(sp, h, "h_out", 32)
                apart(sp)
                need(sp, h, "v_out", 16 * NT)
                apart(sp)

            head(0, False)
            with sp.Fori(1, HEADS - 1) as h:
                head(h, False)
            head(HEADS - 1, True)

            need(sp, HEADS - 1, "mix_out0", 16 * EVEN)
            apart(sp)
            need(sp, HEADS - 1, "mix_out1", 16 * ODD)
            apart(sp)
            sp.dma_start(gains[:, :], final_g.rearrange("(o d) -> o d", o=1).to_broadcast([P, D_MODEL])
                         ).then_inc(S["gains_in"], 16)

            def load_heads(i, par):
                if not (isinstance(i, int) and i == 0):
                    sp.wait_ge(S["fo_t"], 2 * i + (par - 1))
                    apart(sp)
                sp.dma_start(scores[:, 0, 1024 * par:1024 * par + 1024],
                             mix[bass.ds(2 * i + par, 1)].rearrange("o p b h c -> (o p) (b h c)")
                             ).then_inc(S[f"mixin{par}"], 16)

            def load_rows(i, par):
                sp.dma_start(scores[:, 1, 1024 * par:1024 * par + 1024], flat(x_rows[bass.ds(2 * i + par, 1)])
                             ).then_inc(S[f"rowsin{par}"], 16)

            def epi_store(i, par):
                sp.wait_ge(S["fo_y"], 2 * i + (par + 1))
                apart(sp)
                sp.dma_start(flat(y_rows[bass.ds(2 * i + par, 1)]), xn[:, par, :]).then_inc(S[f"y_out{par}"], 16)

            for par in range(2):
                load_heads(0, par)
            for par in range(2):
                load_rows(0, par)
            for par in range(2):
                load_heads(1, par)
            with sp.Fori(0, PAIRS - 2) as i:
                for par in range(2):
                    epi_store(i, par)
                    load_rows(i + 1, par)
                    load_heads(i + 2, par)
            epi_store(PAIRS - 2, 0)
            load_rows(PAIRS - 1, 0)
            load_heads(PAIRS, 0)
            epi_store(PAIRS - 2, 1)
            load_rows(PAIRS - 1, 1)
            epi_store(PAIRS - 1, 0)
            sp.dma_start(scores[0:DEC, 1, 0:1024], x_sample[0]).then_inc(S["rowsin0"], 16)
            epi_store(PAIRS - 1, 1)
            sp.wait_ge(S["fo_y"], NT)
            sp.dma_start(y_sample[0], xn[0:DEC, 0, :]).then_inc(S["y_out0"], 16)
            past(sp, "y_out0", 16 * EVEN)
            apart(sp)
            past(sp, "y_out1", 16 * ODD)
            apart(sp)
            need(sp, HEADS - 1, "k_out0", 16 * EVEN)
            apart(sp)
            need(sp, HEADS - 1, "k_out1", 16 * ODD)
            apart(sp)

        @block.tensor
        def _(pe):
            mm, tr = nc.tensor.matmul, nc.tensor.transpose
            pe.wait_ge(S["masks_ready"], 1)

            prime(pe, "tensor")

            def x_transposes(t):
                pe.wait_ge(S["x_rows"], t + 1)
                if t >= 2:
                    need(pe, 0, "t_evac", t_use["k", t - 2] + 1)
                if t > 0:
                    pe.wait_ge(S["x_lo"], t)
                for kt in range(KT):
                    last = tr(tb[:, kt // 4, P * (kt % 4):P * (kt % 4) + P], x_norm[:, P * kt:P * kt + P],
                              ident[:, :])
                last.then_inc(S["x_t"], 1)

            x_transposes(0)
            x_transposes(1)

            def project(h, t, first):
                units = qk_units(t - 1) if t > 0 else []
                slot = t % XRING
                if first:
                    pe.wait_ge(S["x_hi"], t + 1)
                    pe.wait_ge(S["x_lo"], t + 1)
                else:
                    pe.wait_ge(S[f"xr_in{slot}"], (h - 1) * (16 * XR_PER[slot]) + 16 * (t // XRING + 1))
                for b in (1, 0):
                    if b == 0 and t > 0:
                        rec_scores(h, t - 1)
                    need(pe, h, ("qk_split", "pb_free")[b], t)
                    for kt in range(KT):
                        if t == 0 and b == 1:
                            name, n = lo_of(kt)
                            need(pe, h, "w_hi_ready", kt + 1)
                            need(pe, h, name, n)
                        for part in range(2):
                            x = xr[:, slot, part, kt, :]
                            for w in ((w_hi, w_lo) if part == 0 else (w_hi,)):
                                last = mm(pab[:, b, :], x, w[:, kt, 512 * b:512 * b + 512],
                                          start=(kt == 0 and part == 0 and w is w_hi),
                                          stop=(kt == KT - 1 and part == 1))
                        if t == SAMPLE and b == 0 and kt < KT - 1:
                            last.then_inc(S["w_freed"], 1)
                        if b == 1 and kt >= 1:
                            if first and kt == 2 and 1 <= t < NT - 1:
                                x_transposes(t + 1)
                            for c, m in units[kt - 1:kt]:
                                qk(h, t - 1, c, m)
                    last.then_inc(S[("proj_done", "proj_b")[b]], 1)
                    if b == 1:
                        for c, m in units[KT - 1:]:
                            qk(h, t - 1, c, m)

            def rec_scores(h, t):
                n = P if t < PT else DEC
                need(pe, h, "k_decayed", t + 1)
                need(pe, h, "q_decayed", t + 1)
                for part, blocks in enumerate((range(1, 5), range(5, NS))):
                    u = qk_use["rec", t, part]
                    need(pe, h, "qk_free", u - 1)
                    for j, b in enumerate(blocks):
                        q = NS - 2 if b == 1 else b - 2
                        last = mm(qkb[:, u % 2, P * j:P * j + P], kl[:, b, :], ql[:, q, :], start=True, stop=True)
                last.then_inc(S["kscore_done"], 1)
                need(pe, h, "fin_done", t)
                apart(pe)
                tr(oar[0:n, 1, 256:384], kl[:, 0, 0:n], ident[:, :]).then_inc(S["kd_t"], 1)

            def rec_output(h, t):
                n = P if t < PT else DEC
                need(pe, h, "kd_evac", t + 1)
                need(pe, h, "rec_acc", t + 1)
                if t == 0:
                    need(pe, h, "head_set", 1)
                if t == SAMPLE:
                    need(pe, h, "cache_in", 48)
                s_in = state if t < PT else state_s
                mm(oar[:, 1, 0:P], st[:, :], vr[:, t % 2, :], start=True, stop=False)
                mm(oar[:, 1, 0:P], ql[:, NS - 1, :], s_in[:, :], start=False, stop=True)
                mm(oar[:, 1, P:2 * P], kd[0:n, :], vr[0:n, t % 2, :], start=True, stop=True
                   ).then_inc(S["rec_out"], 1)

            def attend(h, t, first):
                need(pe, h, "combined", t + 1)
                if t == SAMPLE:
                    need(pe, h, "cache_in", 48)
                need(pe, h, "fin_done", t)
                chunks = chunks_of(t)

                if first and t + 2 < NT:
                    pe.wait_ge(S["x_lo"], t + 3)

                def transposes(c):
                    u = t_use["at", t, c]
                    need(pe, h, "t_evac", u - 1)
                    apart(pe)
                    for b, _, n in blocks_of(t, c):
                        last = tr(tb[0:n, u % 2, b:b + P], scores[:, 0, chunks[c][2] + b:chunks[c][2] + b + n],
                                  ident[:, :])
                    last.then_inc(S["at_t"], 1)

                def values(c):
                    u = t_use["at", t, c]
                    need(pe, h, "t_evac", u + 1)
                    blocks = blocks_of(t, c)
                    for j, (b, slot, n) in enumerate(blocks):
                        last = mm(oar[:, 0, 0:VD], at[0:n, u % 2, b:b + P], vv[0:n, slot, :],
                                  start=(c == 0 and j == 0), stop=(c == len(chunks) - 1 and j == len(blocks) - 1))
                    return last

                transposes(0)
                for c in range(len(chunks)):
                    if c + 1 < len(chunks):
                        transposes(c + 1)
                    last = values(c)
                last.then_inc(S["pv_done"], 1)

            def transpose_recurrence(h, t, first):
                if first and t > 0 and t + 1 < NT:
                    pe.wait_ge(S["x_lo"], t + 2)
                u = t_use["rec", t]
                need(pe, h, "t_evac", u - 1)
                need(pe, h, "nat_b", t + 1)
                tr(tb[:, u % 2, 0:P], nb[:, 0, :], ident[:, :])
                tr(tb[:, u % 2, P:2 * P], rc[:, 1, :], ident[:, :])
                tr(tb[:, u % 2, 2 * P:3 * P], nb[:, 1, :], ident[:, :]).then_inc(S["rect_t"], 1)

            def transpose_qk(h, t):
                u = t_use["q", t]
                need(pe, h, "t_evac", u - 1)
                need(pe, h, "qk_split", t + 1)
                for j in range(4):
                    last = tr(tb[:, u % 2, P * j:P * j + P], qn[:, j, :].bitcast(f32), ident[:, :])
                last.then_inc(S["q_t"], 1)
                u = t_use["k", t]
                need(pe, h, "t_evac", u - 1)
                if t == SAMPLE:
                    need(pe, h, "cache_split", 1)
                    for j in range(4):
                        last = tr(tb[:, u % 2, P * j:P * j + P], qn[:, (6, 4, 7, 5)[j], :].bitcast(f32), ident[:, :])
                else:
                    for j in range(2):
                        last = tr(tb[:, u % 2, P * j:P * j + P], qn[:, 4 + j, :].bitcast(f32), ident[:, :])
                last.then_inc(S["k_t"], 1)

            def qk_units(t):
                return [(c, m) for c in range(len(chunks_of(t))) for m in range(2)]

            def qk(h, t, c, m):
                if c == 0:
                    need(pe, h, "t_evac", t_use["k", t] + 1)
                k0, w, _ = chunks_of(t)[c]
                u = qk_use["qk", t, c, m]
                need(pe, h, "qk_free", u - 1)
                for part in range(2):
                    last = mm(qkb[:, u % 2, 0:w], q2[:, m, part, :], kp[:, m, k0:k0 + w],
                              start=(part == 0), stop=(part == 1))
                last.then_inc(S["qk_done"], 1)

            def head(h, first):
                for t in range(NT + 1):
                    if t < NT:
                        project(h, t, first)
                    else:
                        for c, m in qk_units(t - 1):
                            qk(h, t - 1, c, m)
                        rec_scores(h, t - 1)
                    if t > 0:
                        rec_output(h, t - 1)
                    if t < NT:
                        transpose_recurrence(h, t, first)
                    if t > 0:
                        attend(h, t - 1, first)
                    if t < NT:
                        transpose_qk(h, t)

            head(0, True)
            with pe.Fori(1, HEADS) as h:
                head(h, False)

            def epi_transposes(i, par):
                pe.wait_ge(S[f"mixin{par}"], 16 * i + 16)
                if isinstance(i, int) and i == 0 and par == 0:
                    pass
                else:
                    pe.wait_ge(S["fo_lo"], 2 * i + par)
                for kt in range(KT):
                    last = tr(tb[:, kt // 4, P * (kt % 4):P * (kt % 4) + P],
                              scores[:, 0, 1024 * par + P * kt:1024 * par + P * kt + P], ident[:, :])
                last.then_inc(S["fo_t"], 1)

            def epi_project(i, par):
                pe.wait_ge(S["fo_lo"], 2 * i + (par + 1))
                past(pe, "fo_add", 2 * i + (par - 1))
                bank = (pab, qkb)[par]
                for kt in range(KT):
                    for part in range(2):
                        x = xr[:, par, part, kt, :]
                        for w in ((w_hi, w_lo) if part == 0 else (w_hi,)):
                            for b in range(2):
                                last = mm(bank[:, b, :], x, w[:, kt, 512 * b:512 * b + 512],
                                          start=(kt == 0 and part == 0 and w is w_hi),
                                          stop=(kt == KT - 1 and part == 1))
                last.then_inc(S["fo_mm"], 1)

            need(pe, HEADS - 1, "fin_done", NT)
            need(pe, HEADS - 1, "t_evac", T_USES)
            need(pe, HEADS - 1, "qk_free", QK_USES)
            need(pe, HEADS, "w_hi_ready", KT)
            need(pe, HEADS, "w_lo_vec", LO_PER["w_lo_vec"])
            need(pe, HEADS, "w_lo_pool", LO_PER["w_lo_pool"])
            epi_transposes(0, 0)
            with pe.Fori(0, PAIRS) as i:
                epi_transposes(i, 1)
                epi_project(i, 0)
                epi_transposes(i + 1, 0)
                epi_project(i, 1)
            epi_project(PAIRS, 0)

        @block.scalar
        def _(act):
            F = nc.scalar.activation
            prime(act, "scalar")
            nc.scalar.preload_act_table_set("natural_log_exp_and_others")

            def x_square(t):
                act.wait_ge(S["x_in"], 16 * t + 16)
                if t > 0:
                    act.wait_ge(S["x_t"], t)
                F(x_norm, x_raw, ACT.Square, accum_out=tsq[:, 0:1]).then_inc(S["x_sq"], 1)

            def x_high(t):
                act.wait_ge(S["x_t"], t + 1)
                if t >= XRING:
                    act.wait_ge(S[f"xs_out{t % XRING}"], 16 * (t // XRING))
                F(xr[:, t % XRING, 0], tb[:, :, :], ACT.Copy).then_inc(S["x_hi"], 1)

            def split_weights(h, pieces):
                first = isinstance(h, int) and h < 0
                for kt in pieces:
                    if not first:
                        if kt < KT - 1:
                            need(act, h, "w_freed", kt + 1)
                        else:
                            need(act, h, "proj_done", NT)
                    act.wait_ge(S[f"raw_in{kt % RAWRING}"], (h + 1) * 32 + (16 * (kt // RAWRING) + 16))
                    F(w_hi[:, kt, :], (w_raw0 if first else w_raw)[:, kt % RAWRING, :], ACT.Copy
                      ).then_inc(S["w_hi_ready"], 1)

            x_square(0)
            x_high(0)
            x_square(1)
            x_high(1)
            split_weights(-1, range(KT))
            act.wait_ge(S["lam_dots"], 2)
            F(lam[:, 2:4], lam[:, 0:2], ACT.Exp).then_inc(S["setup_exp"], 1)
            act.wait_ge(S["lb_shifted"], 2)
            F(lbw[:, 2:4, :], lbw[:, 0:2, :], ACT.Exp).then_inc(S["setup_exp"], 1)

            def copy_decayed_keys(h, t):
                n = P if t < PT else DEC
                need(act, h, "kd_t", t + 1)
                F(kd[0:n, :], oar[0:n, 1, 256:384], ACT.Copy).then_inc(S["kd_evac"], 1)

            def attention_columns(h, t):
                need(act, h, "proj_done", t + 1)
                pa = pab[:, 0, :]
                q_out = qn[:, 0:4, :].rearrange("p (m a) (d e) -> p m a d e", m=2, d=2)[:, :, 0]
                q_in = pa[:, 0:P].rearrange("p (m e) -> p m e", m=2).unsqueeze(2).to_broadcast([P, 2, 2, HD])
                F(q_out, q_in, ACT.Copy)
                F(qn[:, 4:6, 0:HD], pa[:, P:2 * P].rearrange("p (m e) -> p m e", m=2), ACT.Copy)
                need(act, h, f"k_out{t % 2}", 16 * (t // 2))
                F(kn[:, t % 2, :], pa[:, P:2 * P], ACT.Copy)
                if t == 0:
                    need(act, h, "v_out", 0)
                F(vv[:, slot_of(t), :], pa[:, 2 * P:3 * P], ACT.Copy)
                F(zz[:, 0, :], pa[:, 3 * P:4 * P], ACT.Copy)
                F(ez[:, 0, :], pa[:, 3 * P:4 * P], ACT.Exp, scale=-1.0).then_inc(S["a_evac"], 1)

            def recurrence_columns(h, t):
                need(act, h, "proj_b", t + 1)
                pb = pab[:, 1, :]
                F(fb[:, :, :].rearrange("p g c -> p (g c)"), pb[:, 0:2 * P], ACT.Exp, scale=-1.0)
                F(vr[:, t % 2, :], pb[:, 2 * P:3 * P], ACT.Copy)
                need(act, h, "gates", t)
                F(zz[:, 1, :], pb[:, 3 * P:4 * P], ACT.Copy)
                F(ez[:, 1, :], pb[:, 3 * P:4 * P], ACT.Exp, scale=-1.0).then_inc(S["b_evac"], 1)

            def copy_weights(h, t):
                for c in range(len(chunks_of(t))):
                    if t == SAMPLE - 1:
                        split_weights(h, (c,))
                    u = t_use["at", t, c]
                    w = P * len(blocks_of(t, c))
                    need(act, h, "at_t", at_index[t, c] + 1)
                    F(at[:, u % 2, 0:w], tb[:, u % 2, 0:w], ACT.Copy).then_inc(S["t_evac"], 1)

            def sum_squares(h, t):
                need(act, h, "rec_out", t + 1)
                need(act, h, "pv_done", t + 1)
                F(junk[:, 0:P], oar[:, 0, 0:P], ACT.Square, scale=rsum[:, 0:1], accum_out=ssq[:, 0:1])
                F(junk[:, P:2 * P], oar[:, 1, 0:P], ACT.Square, accum_out=ssq[:, 1:2]).then_inc(S["sumsq"], 1)

            def copy_recurrence(h, t):
                u = t_use["rec", t]
                need(act, h, "rect_t", t + 1)
                F(lf[:, :], tb[:, u % 2, P:2 * P], ACT.Ln, scale=lbh[:, 1:2], bias=lbh[:, 0:1])
                F(qt[:, :], tb[:, u % 2, 0:P], ACT.Copy)
                F(kt_[:, :], tb[:, u % 2, 2 * P:3 * P], ACT.Copy, scale=lbh[:, 1:2]).then_inc(S["t_evac"], 1)

            def copy_qk(h, t):
                u = t_use["q", t]
                need(act, h, "q_t", t + 1)
                F(q2[:, :, :, :].rearrange("p m a c -> p (m a c)"), tb[:, u % 2, :], ACT.Copy
                  ).then_inc(S["t_evac"], 1)
                u = t_use["k", t]
                need(act, h, "k_t", t + 1)
                first, w = (slot_of(t) * P, P) if t < PT else (CACHE_SLOT * P, 2 * P)
                F(kp[:, :, first:first + w], tb[:, u % 2, 0:2 * w].rearrange("p (m c) -> p m c", m=2), ACT.Copy
                  ).then_inc(S["t_evac"], 1)

            def softmax_exp(h, t):
                n = keys_of(t)[1]
                need(act, h, "neg_max", t + 1)
                for m in range(2):
                    last = F(scores[:, m, 0:n], scores[:, m, 0:n], ACT.Exp, bias=nmx[:, m:m + 1], scale=SCALE,
                             accum_out=sums[:, m:m + 1])
                last.then_inc(S["prob_ready"], 1)

            def decay_exp(h, t):
                need(act, h, "dist_ready", t + 1)
                need(act, h, "fin_done", t)
                F(xx[:, :, :], dd[:, :, :], ACT.Exp).then_inc(S["decay_ready"], 1)

            def head(h, first):
                for t in range(NT + 1):
                    if exp_first(t):
                        softmax_exp(h, t - 1)
                    if t < NT:
                        recurrence_columns(h, t)
                    if t > 0 and not exp_first(t):
                        softmax_exp(h, t - 1)
                    if first and t + 2 < NT:
                        x_square(t + 2)
                    if t > 0:
                        copy_decayed_keys(h, t - 1)
                    if t < NT:
                        attention_columns(h, t)
                        if t == 0:
                            need(act, h, "head_set", 1)
                        copy_recurrence(h, t)
                    if t > 0:
                        copy_weights(h, t - 1)
                        sum_squares(h, t - 1)
                    if t < NT:
                        copy_qk(h, t)
                        decay_exp(h, t)
                    if t == SAMPLE:
                        split_weights(h, range(4, KT))
                    if first and t + 2 < NT:
                        x_high(t + 2)

            head(0, True)
            with act.Fori(1, HEADS) as h:
                head(h, False)

            def epi_hi(i, par):
                act.wait_ge(S["fo_t"], 2 * i + (par + 1))
                past(act, "fo_mm", 2 * i + (par - 1))
                F(xr[:, par, 0], tb[:, :, :], ACT.Copy).then_inc(S["fo_hi"], 1)

            def epi_square(i, par):
                past(act, "fo_add", 2 * i + (par + 1))
                F(junk_rows[par], scores[:, 1, 1024 * par:1024 * par + 1024], ACT.Square,
                  accum_out=tsq[:, par:par + 1]).then_inc(S["fo_sq"], 1)

            epi_hi(0, 0)
            with act.Fori(0, PAIRS) as i:
                epi_hi(i, 1)
                epi_square(i, 0)
                epi_hi(i + 1, 0)
                epi_square(i, 1)
            epi_square(PAIRS, 0)

        @block.vector
        def _(dve):
            v = nc.vector
            tt, stt, ts = v.tensor_tensor, v.scalar_tensor_tensor, v.tensor_scalar
            prime(dve, "vector")
            setup = [0]

            def setup_link(ins):
                setup[0] += 1
                ins.then_inc(S["vec_setup"], 1)
                dve.wait_ge(S["vec_setup"], setup[0])

            def x_normalise(t):
                dve.wait_ge(S["x_rs"], t + 1)
                stt(x_norm, x_raw, trs[:, 0:1], x_gain, ALU.mult, ALU.mult).then_inc(S["x_rows"], 1)

            def x_low(t):
                dve.wait_ge(S["x_hi"], t + 1)
                tt(xr[:, t % XRING, 1].rearrange("p k c -> p (k c)"), tb[:, :, :].rearrange("p b c -> p (b c)"),
                   xr[:, t % XRING, 0].rearrange("p k c -> p (k c)").bitcast(f32), ALU.subtract
                   ).then_inc(S["x_lo"], 1)

            def split_weights(h, pieces):
                raw = w_raw0 if isinstance(h, int) and h < 0 else w_raw
                for kt in pieces:
                    if kt not in LO_POOL:
                        need(dve, h + 1, "w_hi_ready", kt + 1)
                        tt(w_lo[:, kt, :], raw[:, kt % RAWRING, :], w_hi[:, kt, :].bitcast(f32), ALU.subtract
                           ).then_inc(S["w_lo_vec"], 1)

            v.memset(ones[:, :], 1.0)
            dve.wait_ge(S["gains_in"], 16)
            x_normalise(0)
            x_low(0)
            x_normalise(1)
            x_low(1)
            split_weights(-1, range(KT))
            dve.wait_ge(S["const_in"], 80)
            for j in range(2):
                v.tensor_tensor_reduce(out=nb[:, j, 0:HD], in0=lamv[:, 2 * j, :], in1=lamv[:, 2 * j + 1, :], scale=1.0,
                                       scalar=0.0, op0=ALU.mult, op1=ALU.add, accum_out=lam[:, j:j + 1]
                                       ).then_inc(S["lam_dots"], 1)
            setup_link(tt(lb[:, :], lbr[:, 0, :], lbr[:, 1, :], ALU.max))
            for r in range(2):
                tt(lbw[:, r, :], lbr[:, r, :], lb[:, :], ALU.subtract).then_inc(S["lb_shifted"], 1)
            dve.wait_ge(S["setup_exp"], 2)
            setup_link(tt(lam[:, 4:5], lam[:, 3:4], lam[:, 2:3], ALU.subtract))
            setup_link(v.tensor_scalar_add(lam[:, 5:6], lam[:, 4:5], -LAM_INIT))
            setup_link(tt(lb[:, :], lbw[:, 2, :], lbw[:, 3, :], ALU.add))
            setup_link(v.reciprocal(oml[:, :], lb[:, :]))
            setup_link(tt(lb[:, :], lbw[:, 2, :], oml[:, :], ALU.mult))
            setup_link(tt(oml[:, :], lbw[:, 3, :], oml[:, :], ALU.mult))
            setup_link(ts(gains2[:, 0, :], gains2[:, 0, :], 1.0 - LAM_INIT, None, ALU.mult))
            dve.wait_ge(S["table_ready"], 2)
            setup_link(stt(bias[:, :], bias[:, :], -1.0, bias[:, :], ALU.mult, ALU.min))
            v.memset(bias[0:CHUNK, SEQ - CHUNK:SEQ], MASKED).then_inc(S["vec_setup"], 1)

            chain = [0]

            def link(h, ins):
                chain[0] += 1
                ins.then_inc(S["vec_chain"], 1)
                need(dve, h, "vec_chain", chain[0])

            def head_start(h):
                need(dve, h, "h_out", 0)
                v.memset(state[:, :], 0.0)
                v.tensor_copy(lbh[:, 0:1], lb[:, bass.ds(h, 1)])
                v.tensor_copy(lbh[:, 1:2], oml[:, bass.ds(h, 1)]).then_inc(S["head_set"], 1)

            def sum_scores(h, t):
                need(dve, h, "kscore_done", t + 1)
                for part, (a, b) in enumerate(((0, 4), (4, NS - 1))):
                    u = qk_use["rec", t, part]
                    tt(masked[:, a:b, :], qkb[:, u % 2, 0:P * (b - a)].rearrange("p (l c) -> p l c", c=P),
                       causal[:, a:b, :], ALU.mult).then_inc(S["qk_free"], 1)
                need(dve, h, "qk_free", u + 1)
                v.tensor_reduce(st[:, :], masked[:, :, :].rearrange("p l c -> p c l"), AX.X, ALU.add
                                ).then_inc(S["rec_acc"], 1)

            def attention_columns(h, t):
                need(dve, h, "a_evac", t + 1)
                pa = pab[:, 0, :]
                q_blocks = qn[:, 0:4, :].rearrange("p (m a) (d e) -> p m a d e", m=2, d=2)
                q_in = pa[:, 0:P].rearrange("p (m e) -> p m e", m=2).unsqueeze(2).to_broadcast([P, 2, 2, HD])
                tt(q_blocks[:, :, 1], q_in, q_blocks[:, :, 0].bitcast(f32), ALU.subtract)
                tt(qn[:, 4:6, HD:P], pa[:, P:2 * P].rearrange("p (m e) -> p m e", m=2),
                   qn[:, 4:6, 0:HD].bitcast(f32), ALU.subtract).then_inc(S["qk_split"], 1)
                if t == SAMPLE:
                    need(dve, h, "cache_in", 48)
                    k_in = kc[:, :].rearrange("p (m e) -> p m e", m=2)
                    link(h, v.tensor_copy(qn[:, 6:8, 0:HD], k_in))
                    tt(qn[:, 6:8, HD:P], k_in, qn[:, 6:8, 0:HD].bitcast(f32), ALU.subtract
                       ).then_inc(S["cache_split"], 1)

            def recurrence_columns(h, t):
                need(dve, h, "b_evac", t + 1)
                ts(rc[:, 1, :], fb[:, 1, :], FMAX, 1.0, ALU.min, ALU.add)
                link(h, v.tensor_scalar_add(rc[:, 0, :], fb[:, 0, :], 1.0))
                link(h, v.reciprocal(rc[:, :, :], rc[:, :, :]))
                tt(nb[:, 0, :], pab[:, 1, 0:P], rc[:, 0, :], ALU.mult).then_inc(S["pb_free"], 1)
                stt(nb[:, 1, :], fb[:, 1, :], FMAX, rc[:, 1, :], ALU.min, ALU.mult).then_inc(S["nat_b"], 1)

            def gate_sigmoids(h, t):
                link(h, v.tensor_scalar_add(ez[:, :, :], ez[:, :, :], 1.0))
                v.reciprocal(ez[:, :, :], ez[:, :, :]).then_inc(S["z_ready"], 1)

            def finish(h, t):
                need(dve, h, "rs_ready", t + 1)
                need(dve, h, "gates", t + 1)
                need(dve, h, f"mix_out{t % 2}", 16 * (t // 2))
                stt(mx[:, t % 2, 0, :], oar[:, 0, 0:P], rsa[:, 0:1], gate[:, t % 2, 0, :], ALU.mult, ALU.mult)
                s, at_last = (state, P - 1) if t < PT else (state_s, DEC - 1)
                stt(s[:, :], s[:, :], xx[:, NX - 1, at_last:at_last + 1], oar[:, 1, P:2 * P], ALU.mult, ALU.add)
                stt(mx[:, t % 2, 1, :], oar[:, 1, 0:P], rs[:, 1:2], gate[:, t % 2, 1, :], ALU.mult, ALU.mult
                    ).then_inc(S["fin_done"], 1)

            def accumulate_decay(h, t):
                need(dve, h, "t_evac", t_use["rec", t] + 1)
                v.tensor_tensor_scan(dd[:, NX - 1, :], ones[:, :], lf[:, :], 0.0, ALU.mult, ALU.add
                                     ).then_inc(S["cum_ready"], 1)

            def biased_scores(h, t):
                chunks = chunks_of(t)
                zero = SEQ - P - P * (t if t < PT else 1)
                for c, (_, w, off) in enumerate(chunks):
                    for m in range(2):
                        u = qk_use["qk", t, c, m]
                        need(dve, h, "qk_done", qk_index[t, c, m] + 1)
                        if c > 0:
                            need(dve, h, "qk_free", u - 1)
                        apart(dve)
                        v.tensor_tensor_reduce(
                            out=scores[:, m, off:off + w], in0=qkb[:, u % 2, 0:w],
                            in1=bias[:, zero + off:zero + off + w], scale=1.0,
                            scalar=(mxs[:, m, c - 1:c] if c else -3e38), op0=ALU.add, op1=ALU.max,
                            accum_out=mxs[:, m, c:c + 1]).then_inc(S["qk_free"], 1)
                    if c == 0:
                        apply_decay(h, t)
                need(dve, h, "qk_free", u + 1)
                ts(nmx[:, :], mxs[:, :, len(chunks) - 1], -SCALE, None, ALU.mult).then_inc(S["neg_max"], 1)

            def combine(h, t):
                n = keys_of(t)[1]
                need(dve, h, "prob_ready", t + 1)
                link(h, v.reciprocal(rsum[:, :], sums[:, :]))
                link(h, stt(cneg[:, :], sums[:, 0:1], rsum[:, 1:2], lam[:, 5:6], ALU.mult, ALU.mult))
                stt(scores[:, 0, 0:n], scores[:, 1, 0:n], cneg[:, 0:1], scores[:, 0, 0:n], ALU.mult, ALU.add
                    ).then_inc(S["combined"], 1)

            def apply_decay(h, t):
                need(dve, h, "decay_ready", t + 1)
                tt(kl[:, :, :], kt_[:, :].unsqueeze(1).to_broadcast([P, NS, P]), xx[:, 0:NS, :], ALU.mult
                   ).then_inc(S["k_decayed"], 1)

            def head(h, first):
                chain[0] = 0
                head_start(h)
                for t in range(NT + 1):
                    if exp_first(t):
                        combine(h, t - 1)
                    if t < NT:
                        recurrence_columns(h, t)
                    if t > 0:
                        sum_scores(h, t - 1)
                    if t > 0 and not exp_first(t):
                        combine(h, t - 1)
                    if first and t + 2 < NT:
                        x_normalise(t + 2)
                    if t < NT:
                        attention_columns(h, t)
                        accumulate_decay(h, t)
                        gate_sigmoids(h, t)
                    if t == SAMPLE:
                        split_weights(h, range(4))
                    if t > 0:
                        finish(h, t - 1)
                    if t < NT:
                        biased_scores(h, t)
                    if t == SAMPLE:
                        split_weights(h, range(4, KT))
                    if first and t + 2 < NT:
                        x_low(t + 2)
                ts(bias[:, :], bias[:, :], 0.25, None, ALU.mult)

            head(0, True)
            with dve.Fori(1, HEADS) as h:
                head(h, False)
            assert chain[0] == PER["vec_chain"], chain[0]

            def epi_lo(i, par):
                dve.wait_ge(S["fo_hi"], 2 * i + (par + 1))
                tt(xr[:, par, 1].rearrange("p k c -> p (k c)"), tb[:, :, :].rearrange("p b c -> p (b c)"),
                   xr[:, par, 0].rearrange("p k c -> p (k c)").bitcast(f32), ALU.subtract
                   ).then_inc(S["fo_lo"], 1)

            def epi_add(i, par):
                dve.wait_ge(S[f"rowsin{par}"], 16 * i + 16)
                apart(dve)
                dve.wait_ge(S["fo_mm"], 2 * i + (par + 1 + PRIME["fo_mm"]))
                rows = scores[:, 1, 1024 * par:1024 * par + 1024]
                tt(rows, (pab, qkb)[par][:, :, :].rearrange("p b c -> p (b c)"), rows, ALU.add
                   ).then_inc(S["fo_add"], 1)

            def epi_normalise(i, par):
                dve.wait_ge(S["fo_rs"], 2 * i + (par + 1))
                past(dve, f"y_out{par}", 16 * i)
                stt(xn[:, par, :], scores[:, 1, 1024 * par:1024 * par + 1024], trs[:, par:par + 1], gains[:, :],
                    ALU.mult, ALU.mult).then_inc(S["fo_y"], 1)

            dve.wait_ge(S["gains_in"], 32)
            epi_lo(0, 0)
            with dve.Fori(0, PAIRS) as i:
                epi_lo(i, 1)
                epi_add(i, 0)
                epi_normalise(i, 0)
                epi_lo(i + 1, 0)
                epi_add(i, 1)
                epi_normalise(i, 1)
            epi_add(PAIRS, 0)
            epi_normalise(PAIRS, 0)

        @block.gpsimd
        def _(pool):
            g = nc.gpsimd
            prime(pool, "gpsimd")
            setup = [0]

            def setup_link(ins):
                setup[0] += 1
                ins.then_inc(S["pool_setup"], 1)
                pool.wait_ge(S["pool_setup"], setup[0])

            g.memset(half[:, :], -0.5)
            g.memset(ident[:, :], 0.0)
            setup_link(g.memset(causal[:, :, :], 1.0))
            g.affine_select(out=ident[:, :], in_=ident[:, :], compare_op=ALU.not_equal, fill=1.0, base=0,
                            pattern=[[-1, P]], channel_multiplier=1).then_inc(S["masks_ready"], 1)
            table = xx[:, 0:8, :].rearrange("p a c -> p (a c)").bitcast(i32)
            for part in range(2):
                setup_link(g.iota(table, pattern=[[-2, 1024]], base=2 * (SEQ - P - 1024 * part),
                                  channel_multiplier=2))
                g.tensor_copy(bias[:, 1024 * part:1024 * part + 1024], table).then_inc(S["table_ready"], 1)
                pool.wait_ge(S["table_ready"], part + 1)

            def row_scale(ready, signal, n, par):
                pool.wait_ge(S[ready], n)
                apart(pool)
                g.tensor_scalar(tms[:, par:par + 1], tsq[:, par:par + 1], 1.0 / D_MODEL, EPS, ALU.mult, ALU.add
                                ).then_inc(S[signal + "_mean"], 1)
                pool.wait_ge(S[signal + "_mean"], n)
                g.tensor_tensor(trs[:, par:par + 1], tms[:, par:par + 1], half[:, 0:1], ALU.pow
                                ).then_inc(S[signal], 1)

            def split_weights(h):
                raw = w_raw0 if isinstance(h, int) and h < 0 else w_raw
                for kt in LO_POOL:
                    need(pool, h + 1, "w_hi_ready", kt + 1)
                    g.tensor_tensor(w_lo[:, kt, :], raw[:, kt % RAWRING, :], w_hi[:, kt, :].bitcast(f32), ALU.subtract
                                    ).then_inc(S["w_lo_pool"], 1)

            for t in range(2):
                row_scale("x_sq", "x_rs", t + 1, 0)
            split_weights(-1)

            def keep(out, pattern, base, step):
                return g.affine_select(out=out, in_=out, compare_op=ALU.is_ge, fill=0.0, base=base,
                                       pattern=pattern, channel_multiplier=step)

            for j, size in enumerate((BASE,) + tuple(2 * s for s in HALVES)):
                nblk = P // size
                out = causal[:, j, :].rearrange("p (b r) -> p b r", b=nblk)
                setup_link(keep(out, [[-size, nblk], [0, size]], 0, 1))
                if j == 0:
                    setup_link(keep(out, [[size, nblk], [1, size]], 0, -1))
                else:
                    setup_link(keep(out, [[size, nblk], [0, size]], size // 2 - 1, -1))
                    setup_link(keep(out, [[0, nblk], [1, size]], -(size // 2), 0))

            chain = [0]

            def link(h, ins):
                chain[0] += 1
                ins.then_inc(S["pool_chain"], 1)
                need(pool, h, "pool_chain", chain[0])

            def gates(h, t):
                need(pool, h, "z_ready", t + 1)
                link(h, g.tensor_tensor(zz[:, :, :], zz[:, :, :], ez[:, :, :], ALU.mult))
                g.tensor_tensor(gate[:, t % 2, :, :], zz[:, :, :], gains2[:, :, :], ALU.mult).then_inc(S["gates"], 1)

            def apply_decay(h, t):
                need(pool, h, "decay_ready", t + 1)
                g.tensor_tensor(ql[:, :, :], qt[:, :].unsqueeze(1).to_broadcast([P, NS, P]), xx[:, NX - NS:NX, :],
                                ALU.mult).then_inc(S["q_decayed"], 1)

            def head_scales(h, t):
                need(pool, h, "sumsq", t + 1)
                apart(pool)
                link(h, g.tensor_scalar(ms[:, :], ssq[:, :], 1.0 / VD, EPS, ALU.mult, ALU.add))
                link(h, g.tensor_tensor(rs[:, :], ms[:, :], half[:, :], ALU.pow))
                g.tensor_tensor(rsa[:, :], rs[:, 0:1], rsum[:, 0:1], ALU.mult).then_inc(S["rs_ready"], 1)

            def exponents(h, t):
                n = P if t < PT else DEC
                need(pool, h, "cum_ready", t + 1)
                cum = dd[:, NX - 1, :]
                sub = ALU.subtract
                for j, s in enumerate(HALVES):
                    c = cum.rearrange("p (b a r) -> p b a r", a=2, r=s)
                    o = dd[:, 2 + j, :].rearrange("p (b a r) -> p b a r", a=2, r=s)
                    ref = c[:, :, 0, s - 1:s].to_broadcast([P, P // (2 * s), s])
                    g.tensor_tensor(o[:, :, 0, :], ref, c[:, :, 0, :], sub)
                    g.tensor_tensor(o[:, :, 1, :], c[:, :, 1, :], ref, sub)
                c = cum.rearrange("p (b r) -> p b r", r=BASE)
                ref = c[:, :, 1:2].to_broadcast([P, P // BASE, BASE])
                g.tensor_tensor(dd[:, 1, :].rearrange("p (b r) -> p b r", r=BASE), ref, c, sub)
                g.tensor_tensor(dd[:, NX - 2, :].rearrange("p (b r) -> p b r", r=BASE), c, ref, sub)
                g.tensor_tensor(dd[:, 0, 0:n], cum[:, n - 1:n].to_broadcast([P, n]), cum[:, 0:n], sub
                                ).then_inc(S["dist_ready"], 1)

            def head(h, first):
                chain[0] = 0
                for t in range(NT + 1):
                    if first and t + 2 < NT:
                        row_scale("x_sq", "x_rs", t + 3, 0)
                    if t < NT:
                        exponents(h, t)
                    if t > 0:
                        head_scales(h, t - 1)
                    if t < NT:
                        apply_decay(h, t)
                        gates(h, t)
                    if t == SAMPLE:
                        split_weights(h)

            head(0, True)
            with pool.Fori(1, HEADS) as h:
                head(h, False)
            assert chain[0] == PER["pool_chain"]

            with pool.Fori(0, PAIRS) as i:
                for par in range(2):
                    row_scale("fo_sq", "fo_rs", 2 * i + (par + 1), par)
            row_scale("fo_sq", "fo_rs", NT, 0)


_INS = ["x_prompt", "x_sample", "cache_k", "cache_v", "state_h", "norm_g", "w_in", "lambda_qk", "subln_g", "rec_lb",
        "rec_norm_g", "w_out", "final_g"]
_OUTS = [(1, SEQ, D_MODEL), (1, DEC, D_MODEL), (1, 1, SEQ, HEADS, 2 * HD), (1, 1, SEQ, HEADS, VD),
         (1, 1, HEADS, VD, VD), (1, 1, DEC, HEADS, 2 * HD), (1, 1, DEC, HEADS, VD), (1, 1, HEADS, VD, VD)]


def kernel(**inputs):
    import concourse.bacc as bacc
    from concourse.bass_utils import run_bass_kernel_spmd

    nc = bacc.Bacc("TRN2", target_bir_lowering=False, num_devices=1)
    arrays, args = {}, []
    for name in _INS:
        a = np.ascontiguousarray(inputs[name])
        arrays[f"in_{name}"] = a
        args.append(nc.dram_tensor(f"in_{name}", a.shape, mybir.dt.from_np(a.dtype), kind="ExternalInput").ap())
    for i, shape in enumerate(_OUTS):
        args.append(nc.dram_tensor(f"out_{i}", shape, mybir.dt.float32, kind="ExternalOutput").ap())
    build(nc, *args)
    r = run_bass_kernel_spmd(nc, [arrays], core_ids=[0])
    return tuple(r.results[0][f"out_{i}"] for i in range(len(_OUTS)))
```

```python
from contextlib import ExitStack

import numpy as np

import concourse.bass as bass
from concourse import mybir

P = 128
D_MODEL = 1024
SEQ = 2048
DEC = 64
PAST = 128
HEADS = 4
HD = 64
VD = 128
CHUNK = 64
KT = D_MODEL // P
PT = SEQ // P
NT = PT + 1
SAMPLE = NT - 1
SLOTS = NT + 1
CACHE_SLOT = PT
HALVES = (64, 32, 16, 8, 4)
BASE = 4
NS = 2 + len(HALVES)
NX = NS + 2
EPS = 1e-6
SCALE = HD ** -0.5
LAM_INIT = 0.2
MASKED = -1e30
FMAX = float(2.0 ** 59)


def slot_of(t):
    return t if t < PT else CACHE_SLOT + 1


def keys_of(t):
    if t < PT:
        return 0, P * (t + 1)
    return CACHE_SLOT * P, PAST + DEC


def chunks_of(t):
    k0, n = keys_of(t)
    return [(k0 + c, min(512, n - c), c) for c in range(0, n, 512)]


def blocks_of(t, c):
    k0, w, _ = chunks_of(t)[c]
    return [(b, (k0 + b) // P, min(P, w - b)) for b in range(0, w, P)]


def lo_of(kt):
    if kt in LO_POOL:
        return "w_lo_pool", LO_POOL.index(kt) + 1
    return "w_lo_vec", kt + 1 - sum(j < kt for j in LO_POOL)


NCH = sum(len(chunks_of(t)) for t in range(NT))
T_USES = NCH + 3 * NT
QK_USES = 2 * NCH + 2 * NT
XRING = 3
RAWRING = 4
LO_POOL = (6,)
LO_PER = dict(w_lo_vec=KT - len(LO_POOL), w_lo_pool=len(LO_POOL))
EVEN, ODD = (NT + 1) // 2, NT // 2
PAIRS = PT // 2


def build(nc, x_prompt, x_sample, cache_k, cache_v, state_h, norm_g, w_in, lambda_qk, subln_g, rec_lb,
          rec_norm_g, w_out, final_g, y_prompt, y_sample, new_k_prompt, new_v_prompt, new_h_prompt,
          new_k_sample, new_v_sample, new_h_sample):
    f32, f32r, i32 = mybir.dt.float32, mybir.dt.float32r, mybir.dt.int32
    ALU, ACT, AX = mybir.AluOpType, mybir.ActivationFunctionType, mybir.AxisListType
    ctx = ExitStack()
    with ctx:
        def sb(name, shape, dt=f32):
            return ctx.enter_context(nc.sbuf_tensor(name, shape, dt))

        def ps(name):
            return ctx.enter_context(nc.psum_tensor(name, [P, 2, 512], f32))

        xs = nc.dram_tensor("xs", [NT, P, 2 * KT * P], f32).ap()
        mix = nc.dram_tensor("mix", [NT, P, 2, HEADS, VD], f32).ap()

        w_hi = sb("w_hi", [P, KT, 1024], f32r)
        w_lo = sb("w_lo", [P, KT, 1024], f32r)
        w_raw = sb("w_raw", [P, RAWRING, 1024])
        xr = sb("xr", [P, XRING, 2, KT, P], f32r)
        kp = sb("kp", [P, 2, SLOTS * P], f32r)
        vv = sb("vv", [P, SLOTS, VD])
        scores = sb("scores", [P, 2, SEQ])
        bias = sb("bias", [P, SEQ])
        at = sb("at", [P, 2, 512])
        qn = sb("qn", [P, 8, P], f32r)
        q2 = sb("q2", [P, 2, 2, P], f32r)
        kn = sb("kn", [P, 2, P])
        zz = sb("zz", [P, 2, P])
        ez = sb("ez", [P, 2, P])
        gate = sb("gate", [P, 2, 2, P])
        fb = sb("fb", [P, 2, P])
        rc = sb("rc", [P, 2, P])
        nb = sb("nb", [P, 2, P])
        vr = sb("vr", [P, 2, P])
        lf = sb("lf", [P, P])
        qt = sb("qt", [P, P])
        kt_ = sb("kt_", [P, P])
        dd = sb("dd", [P, NX, P])
        xx = sb("xx", [P, NX, P])
        total = sb("total", [P, 2])
        kq = sb("kq", [P, 2, NS, P])
        kl, ql = kq[:, 0], kq[:, 1]
        masked = sb("masked", [P, NS - 1, P])
        causal = sb("causal", [P, NS - 1, P])
        st = sb("st", [P, P])
        kd = sb("kd", [P, P])
        state = sb("state", [P, P])
        state_s = sb("state_s", [P, P])
        mx = sb("mx", [P, 2, 2, P])
        junk = sb("junk", [P, 2 * P])
        junk_rows = (at[:, :, :].rearrange("p a c -> p (a c)"),
                     dd[:, 0:8, :].rearrange("p a c -> p (a c)"))
        x_raw = (w_raw[:, 0, :], w_raw[:, 3, :])
        x_norm, x_gain = w_raw[:, 1, :], w_raw[:, 2, :]
        w_raw0 = ([scores[:, m, 1024 * a:1024 * a + 1024] for m in range(2) for a in range(2)]
                  + [vv[:, 8 * a:8 * a + 8, :].rearrange("p k c -> p (k c)") for a in range(2)]
                  + [bias[:, 1024 * a:1024 * a + 1024] for a in range(2)])

        def raw_piece(weights, kt):
            return w_raw0[kt] if isinstance(weights, int) and weights == 0 else w_raw[:, kt % RAWRING, :]

        gains = kq[:, :, :, :].rearrange("p a n c -> p (a n c)")[:, 0:D_MODEL]
        heads_in = bias[:, :].rearrange("p (a c) -> p a c", a=2)
        rows_in = scores[:, 1, :].rearrange("p (a c) -> p a c", a=2)
        xn = vv[:, 0:2 * KT, :].rearrange("p (a k) c -> p a (k c)", a=2)
        kc = sb("kc", [P, P])
        ident = sb("ident", [P, P])
        ones = sb("ones", [P, P])
        gains2 = sb("gains2", [P, 2, P])
        tables = (at[:, :, :].rearrange("p a c -> p (a c)").bitcast(i32), scores[:, 1, 1024:2048].bitcast(i32))
        lamv = masked[:, 0:2, :].rearrange("p a (b d) -> p (a b) d", b=2)
        lbr = sb("lbr", [P, 2, HEADS])
        lbw = sb("lbw", [P, 4, HEADS])
        lb = sb("lb", [P, HEADS])
        oml = sb("oml", [P, HEADS])
        lbh = sb("lbh", [P, 2])
        lam = sb("lam", [P, 6])
        half = sb("half", [P, 2])
        ssq = sb("ssq", [P, 2])
        ms = sb("ms", [P, 2])
        rs = sb("rs", [P, 2])
        tsq = sb("tsq", [P, 2])
        tms = sb("tms", [P, 2])
        trs = sb("trs", [P, 2])
        rsa = sb("rsa", [P, 1])
        mxs = sb("mxs", [P, 2, 4])
        nmx = sb("nmx", [P, 2])
        sums = sb("sums", [P, 2])
        rsum = sb("rsum", [P, 2])
        cneg = sb("cneg", [P, 1])

        pab = ps("pab")
        qkb = ps("qkb")
        tb = ps("tb")
        oar = ps("oar")

        PER = dict(
            w_hi_ready=KT, w_freed=KT - 1, proj_b=NT, proj_done=NT, a_evac=NT, b_evac=NT, qk_split=NT,
            nat_b=NT, pb_free=NT, z_ready=NT, gates=NT, rect_t=NT, q_t=NT, k_t=NT,
            t_evac=T_USES, qk_done=2 * NCH, kscore_done=NT, qk_free=QK_USES, neg_max=NT, prob_ready=NT,
            combined=NCH, at_t=NCH, pv_done=NT, cum_ready=NT, dist_ready=NT, decay_ready=NT, k_decayed=NT,
            q_decayed=NT, kd_t=NT, kd_evac=NT, rec_acc=NT, rec_out=NT, sumsq=NT, rs_ready=NT, fin_done=NT,
            head_set=1, cache_split=1, vec_chain=5 * NT + 1, pool_chain=3 * NT,
            k_out0=16 * EVEN, k_out1=16 * ODD, v_out=16 * NT, mix_out0=16 * EVEN, mix_out1=16 * ODD,
            h_out=16, hs_out=16, cache_in=48, **LO_PER)
        PRIME = dict(qk_split=1, pb_free=1, fin_done=1, qk_free=2, t_evac=2, gates=1,
                     k_out0=16, k_out1=16, v_out=16, mix_out0=16, mix_out1=16, h_out=16,
                     fo_mm=2, fo_add=2, y_out0=16, y_out1=16)
        PRIMED_BY = dict(gpsimd=("gates", "k_out0", "k_out1", "v_out", "mix_out0", "mix_out1", "h_out",
                                 "y_out0", "y_out1"),
                         vector=("qk_split", "pb_free", "fin_done", "qk_free", "fo_add"),
                         scalar=("t_evac",), tensor=("fo_mm",))
        assert sorted(PRIME) == sorted(sum(PRIMED_BY.values(), ()))

        S = {name: ctx.enter_context(nc.semaphore(name)) for name in list(PER) + [
            "x_in0", "x_in1", "gains_in", "const_in", *(f"raw_in{kt}" for kt in range(KT)), "xs_out0",
            "xs_out1", "xs_out2", "xr_in0", "xr_in1", "xr_in2", "y_out0", "y_out1", "mixin0", "mixin1",
            "rowsin0", "rowsin1",
            "x_sq", "x_rs", "x_rs_mean", "x_rows", "x_t", "x_hi", "x_lo", "fo_rs_mean",
            "masks_ready", "table_ready", "lam_dots", "lb_shifted", "setup_exp", "vec_setup", "pool_setup",
            "apart", "fo_t", "fo_hi", "fo_lo", "fo_mm", "fo_add", "fo_sq", "fo_rs", "fo_y"]}

        def need(eng, h, name, n):
            eng.wait_ge(S[name], h * PER[name] + (PRIME.get(name, 0) + n))

        def apart(eng):
            eng.sem_inc(S["apart"], 1)

        def past(eng, name, n):
            eng.wait_ge(S[name], n + PRIME.get(name, 0))

        def prime(engine, who):
            for name in PRIMED_BY[who]:
                engine.sem_inc(S[name], PRIME[name])

        block = ctx.enter_context(nc.Block())

        t_use, qk_use, qk_index, at_index = {}, {}, {}, {}
        for t in range(NT + 1):
            if 0 < t < NT:
                for c in range(len(chunks_of(t - 1))):
                    for m in range(2):
                        qk_use["qk", t - 1, c, m] = len(qk_use)
                        qk_index[t - 1, c, m] = len(qk_index)
            if t > 0:
                for part in range(2):
                    qk_use["rec", t - 1, part] = len(qk_use)
            if t == SAMPLE:
                for m in range(2):
                    qk_use["qk", t, 0, m] = len(qk_use)
                    qk_index[t, 0, m] = len(qk_index)
            if t < NT:
                t_use["rec", t] = len(t_use)
            if t > 0:
                for c in range(len(chunks_of(t - 1))):
                    if t == SAMPLE and c == 2:
                        for what in ("q", "k"):
                            t_use[what, t] = len(t_use)
                    t_use["at", t - 1, c] = len(t_use)
                    at_index[t - 1, c] = len(at_index)
            if t < SAMPLE:
                for what in ("q", "k"):
                    t_use[what, t] = len(t_use)
        assert len(t_use) == T_USES and len(qk_use) == QK_USES and T_USES % 2 == 0 and QK_USES % 2 == 0

        XR_PER = [len(range(s, NT, XRING)) for s in range(XRING)]
        x_rows = x_prompt[0].rearrange("(t p) d -> t p d", p=P)
        y_rows = y_prompt[0].rearrange("(t p) d -> t p d", p=P)

        def flat(ap):
            return ap.rearrange("o p d -> (o p) d")

        @block.sync
        def _(sp):
            def raw_load(weights, kt):
                place = raw_piece(weights, kt)
                if weights is None:
                    sp.dma_start(place, w_out[0, kt * P:(kt + 1) * P, :]).then_inc(S[f"raw_in{kt}"], 16)
                else:
                    rows = w_in[0, kt * P:(kt + 1) * P, :].rearrange("p (g h c) -> p g h c", g=8, h=HEADS)
                    sp.dma_start(place.rearrange("p (g c) -> p g c", g=8),
                                 rows[:, :, bass.ds(weights, 1), :].rearrange("p g o c -> p g (o c)")
                                 ).then_inc(S[f"raw_in{kt}"], 16)

            def rows_load(t):
                if t > 1:
                    sp.wait_ge(S["x_rows"], t - 1)
                name = S[f"x_in{t % 2}"]
                if t < PT:
                    sp.dma_start(x_raw[t % 2], x_rows[t]).then_inc(name, 16)
                else:
                    sp.dma_start(x_raw[0][0:DEC, :], x_sample[0]).then_inc(name, 16)

            def xs_store(t):
                sp.wait_ge(S["x_lo"], t + 1)
                sp.dma_start(xs[t], xr[:, t % XRING].rearrange("p a k c -> p (a k c)").bitcast(f32)
                             ).then_inc(S[f"xs_out{t % XRING}"], 16)

            def x_load(t):
                slot = t % XRING
                sp.dma_start(xr[:, slot].rearrange("p a k c -> p (a k c)").bitcast(f32), xs[t]
                             ).then_inc(S[f"xr_in{slot}"], 16)

            rows_load(0)
            sp.dma_start(x_gain, norm_g[0:1, :].to_broadcast([P, D_MODEL])).then_inc(S["gains_in"], 16)
            for kt in range(2):
                raw_load(0, kt)
            rows_load(1)
            for kt in range(2, KT):
                raw_load(0, kt)
            with nc.allow_non_contiguous_dma(reason="small constants"):
                sp.dma_start(lamv[:, :, :].rearrange("p a d -> p (a d)"),
                             lambda_qk.rearrange("l a d -> l (a d)").to_broadcast([P, 4 * HD])
                             ).then_inc(S["const_in"], 16)
                sp.dma_start(gains2[:, 0, :], subln_g[0:1, :].to_broadcast([P, VD])).then_inc(S["const_in"], 16)
                sp.dma_start(gains2[:, 1, :], rec_norm_g[0:1, :].to_broadcast([P, VD])).then_inc(S["const_in"], 16)
                for r in range(2):
                    sp.dma_start(lbr[:, r, :], rec_lb[r].rearrange("(h d) -> d h", h=HEADS)
                                 ).then_inc(S["const_in"], 16)
            def mix_store(h, t):
                need(sp, h, "fin_done", t + 1)
                apart(sp)
                sp.dma_start(mix[t, :, :, bass.ds(h, 1), :].rearrange("p b o c -> p b (o c)"),
                             mx[:, t % 2, :, :]).then_inc(S[f"mix_out{t % 2}"], 16)
                if t == PT - 1:
                    sp.dma_start(new_h_prompt[0, 0, bass.ds(h, 1)].rearrange("o d v -> (o d) v"), state[:, :]
                                 ).then_inc(S["h_out"], 16)

            def load_heads(i, par):
                if not (isinstance(i, int) and i == 0):
                    sp.wait_ge(S["fo_t"], 2 * i + (par - 1))
                    apart(sp)
                sp.dma_start(heads_in[:, par, :],
                             mix[bass.ds(2 * i + par, 1)].rearrange("o p b h c -> (o p) (b h c)")
                             ).then_inc(S[f"mixin{par}"], 16)

            def head(h, last):
                def one_head(ap):
                    return ap[:, bass.ds(h, 1), :].rearrange("t o d -> t (o d)")

                first = isinstance(h, int) and h == 0
                following = None if last else h + 1

                def raw_ahead(kt):
                    name, n = lo_of(RAWRING + kt)
                    need(sp, h, name, n)
                    apart(sp)
                    raw_load(following, kt)

                def ahead_load(h, done, t):
                    assert (done - 1) % XRING == t
                    if first:
                        sp.wait_ge(S[f"xs_out{t}"], 16 * XR_PER[t])
                    need(sp, h, "proj_done", done)
                    apart(sp)
                    x_load(t)

                for t in range(NT):
                    if first:
                        if t + 2 < NT:
                            rows_load(t + 2)
                        if t == 0:
                            xs_store(0)
                        if t < NT - 1:
                            xs_store(t + 1)
                    elif 1 <= t and t + 2 < NT:
                        need(sp, h, "proj_done", t)
                        apart(sp)
                        x_load(t + 2)
                    if t == 1:
                        if first:
                            need(sp, h, "proj_done", 1)
                        sp.dma_start(kc[:, :], one_head(cache_k[0, 0])).then_inc(S["cache_in"], 16)
                        sp.dma_start(vv[:, CACHE_SLOT, :], one_head(cache_v[0, 0])).then_inc(S["cache_in"], 16)
                        sp.dma_start(state_s[:, :], state_h[0, 0, bass.ds(h, 1)].rearrange("o d v -> (o d) v")
                                     ).then_inc(S["cache_in"], 16)
                    if t == (SAMPLE if first else 2):
                        if first:
                            sp.wait_ge(S["x_t"], NT)
                        for kt in range(RAWRING):
                            raw_ahead(kt)
                    if not last and t >= NT - 2:
                        ahead_load(h, t, 2 if t == NT - 2 else 0)
                    need(sp, h, "a_evac", t + 1)
                    apart(sp)
                    ko, vo = (new_k_prompt, new_v_prompt) if t < PT else (new_k_sample, new_v_sample)
                    r0, n = (t * P, P) if t < PT else (0, DEC)
                    sp.dma_start(one_head(ko[0, 0, r0:r0 + n]), kn[0:n, t % 2, :]).then_inc(S[f"k_out{t % 2}"], 16)
                    sp.dma_start(one_head(vo[0, 0, r0:r0 + n]), vv[0:n, slot_of(t), :]).then_inc(S["v_out"], 16)
                    if 0 < t < SAMPLE:
                        mix_store(h, t - 1)
                for kt in range(RAWRING, KT):
                    name, n = lo_of(kt - RAWRING)
                    need(sp, h + 1, name, n)
                    apart(sp)
                    raw_load(following, kt)
                if not last:
                    ahead_load(h, NT, 1)
                if last:
                    need(sp, h, "neg_max", NT)
                    apart(sp)
                    need(sp, h, "mix_out0", 16 * (EVEN - 1))
                    apart(sp)
                    load_heads(0, 0)
                mix_store(h, SAMPLE - 1)
                if last:
                    need(sp, h, "mix_out1", 16 * ODD)
                    apart(sp)
                    load_heads(0, 1)
                mix_store(h, SAMPLE)
                sp.dma_start(new_h_sample[0, 0, bass.ds(h, 1)].rearrange("o d v -> (o d) v"), state_s[:, :]
                             ).then_inc(S["hs_out"], 16)
                need(sp, h, "h_out", 16)
                apart(sp)
                sp.wait_ge(S["hs_out"], 16 * h + 16)
                apart(sp)
                need(sp, h, "v_out", 16 * NT)
                apart(sp)

            head(0, False)
            with sp.Fori(1, HEADS - 1) as h:
                head(h, False)
            head(HEADS - 1, True)

            need(sp, HEADS - 1, "mix_out0", 16 * EVEN)
            apart(sp)
            sp.dma_start(gains[:, :], final_g.rearrange("(o d) -> o d", o=1).to_broadcast([P, D_MODEL])
                         ).then_inc(S["gains_in"], 16)

            def load_rows(i, par):
                sp.dma_start(rows_in[:, par, :], flat(x_rows[bass.ds(2 * i + par, 1)])
                             ).then_inc(S[f"rowsin{par}"], 16)

            def epi_store(i, par):
                sp.wait_ge(S["fo_y"], 2 * i + (par + 1))
                apart(sp)
                sp.dma_start(flat(y_rows[bass.ds(2 * i + par, 1)]), xn[:, par, :]).then_inc(S[f"y_out{par}"], 16)

            for par in range(2):
                load_rows(0, par)
            for par in range(2):
                load_heads(1, par)
            with sp.Fori(0, PAIRS - 2) as i:
                for par in range(2):
                    epi_store(i, par)
                    load_rows(i + 1, par)
                    load_heads(i + 2, par)
            epi_store(PAIRS - 2, 0)
            load_rows(PAIRS - 1, 0)
            load_heads(PAIRS, 0)
            epi_store(PAIRS - 2, 1)
            load_rows(PAIRS - 1, 1)
            epi_store(PAIRS - 1, 0)
            sp.dma_start(rows_in[0:DEC, 0, :], x_sample[0]).then_inc(S["rowsin0"], 16)
            epi_store(PAIRS - 1, 1)
            sp.wait_ge(S["fo_y"], NT)
            sp.dma_start(y_sample[0], xn[0:DEC, 0, :]).then_inc(S["y_out0"], 16)
            past(sp, "y_out0", 16 * EVEN)
            apart(sp)
            past(sp, "y_out1", 16 * ODD)
            apart(sp)
            need(sp, HEADS - 1, "k_out0", 16 * EVEN)
            apart(sp)
            need(sp, HEADS - 1, "k_out1", 16 * ODD)
            apart(sp)

        @block.tensor
        def _(pe):
            mm, tr = nc.tensor.matmul, nc.tensor.transpose
            pe.wait_ge(S["masks_ready"], 1)

            prime(pe, "tensor")

            def x_transposes(t):
                pe.wait_ge(S["x_rows"], t + 1)
                if t >= 2:
                    need(pe, 0, "t_evac", t_use["k", t - 2] + 1)
                if t > 0:
                    pe.wait_ge(S["x_lo"], t)
                for kt in range(KT):
                    last = tr(tb[:, kt // 4, P * (kt % 4):P * (kt % 4) + P], x_norm[:, P * kt:P * kt + P],
                              ident[:, :])
                last.then_inc(S["x_t"], 1)

            x_transposes(0)

            def project(h, t, first):
                units = qk_units(t - 1) if t > 0 else []
                slot = t % XRING
                if first:
                    pe.wait_ge(S["x_hi"], t + 1)
                    pe.wait_ge(S["x_lo"], t + 1)
                else:
                    pe.wait_ge(S[f"xr_in{slot}"], (h - 1) * (16 * XR_PER[slot]) + 16 * (t // XRING + 1))
                steps = [(b, kt) for b in (1, 0) for kt in range(KT)]
                for b, kt in steps:
                    if kt == 0:
                        need(pe, h, ("qk_split", "pb_free")[b], t)
                    if b == 0 and kt == 6:
                        transpose_recurrence(h, t, first)
                    if b == 0 and kt == 2 and t > 0:
                        rec_scores(h, t - 1)
                    if t == 0 and b == 1:
                        name, n = lo_of(kt)
                        need(pe, h, "w_hi_ready", kt + 1)
                        need(pe, h, name, n)
                    for part in range(2):
                        x = xr[:, slot, part, kt, :]
                        for w in ((w_hi, w_lo) if part == 0 else (w_hi,)):
                            last = mm(pab[:, b, :], x, w[:, kt, 512 * b:512 * b + 512],
                                      start=(kt == 0 and part == 0 and w is w_hi),
                                      stop=(kt == KT - 1 and part == 1))
                    if t == SAMPLE and b == 0 and kt < KT - 1:
                        last.then_inc(S["w_freed"], 1)
                    if b == 1 and kt >= 1:
                        if first and kt == (2 if t > 0 else KT - 1) and t < NT - 1:
                            x_transposes(t + 1)
                        for c, m in units[kt - 1:kt]:
                            qk(h, t - 1, c, m)
                    if b == 0 and kt == 0:
                        for c, m in units[KT - 1:]:
                            qk(h, t - 1, c, m)
                    if kt == KT - 1:
                        last.then_inc(S[("proj_done", "proj_b")[b]], 1)

            def rec_scores(h, t):
                n = P if t < PT else DEC
                need(pe, h, "k_decayed", t + 1)
                need(pe, h, "q_decayed", t + 1)
                for part, blocks in enumerate((range(1, 5), range(5, NS))):
                    u = qk_use["rec", t, part]
                    need(pe, h, "qk_free", u - 1)
                    for j, b in enumerate(blocks):
                        q = NS - 2 if b == 1 else b - 2
                        last = mm(qkb[:, u % 2, P * j:P * j + P], kl[:, b, :], ql[:, q, :], start=True, stop=True)
                last.then_inc(S["kscore_done"], 1)
                need(pe, h, "fin_done", t)
                apart(pe)
                tr(oar[0:n, 1, 256:384], kl[:, 0, 0:n], ident[:, :]).then_inc(S["kd_t"], 1)

            def rec_output(h, t):
                n = P if t < PT else DEC
                need(pe, h, "kd_evac", t + 1)
                need(pe, h, "rec_acc", t + 1)
                if t == 0:
                    need(pe, h, "head_set", 1)
                if t == SAMPLE:
                    need(pe, h, "cache_in", 48)
                s_in = state if t < PT else state_s
                mm(oar[:, 1, 0:P], st[:, :], vr[:, t % 2, :], start=True, stop=False)
                mm(oar[:, 1, 0:P], ql[:, NS - 1, :], s_in[:, :], start=False, stop=True)
                mm(oar[:, 1, P:2 * P], kd[0:n, :], vr[0:n, t % 2, :], start=True, stop=True
                   ).then_inc(S["rec_out"], 1)

            def attend(h, t, first):
                if t == SAMPLE:
                    need(pe, h, "cache_in", 48)
                need(pe, h, "fin_done", t)
                chunks = chunks_of(t)

                if first and t + 2 < NT:
                    pe.wait_ge(S["x_lo"], t + 3)

                def transposes(c):
                    u = t_use["at", t, c]
                    need(pe, h, "t_evac", u - 1)
                    apart(pe)
                    need(pe, h, "combined", at_index[t, c] + 1)
                    apart(pe)
                    for b, _, n in blocks_of(t, c):
                        last = tr(tb[0:n, u % 2, b:b + P], scores[:, 0, chunks[c][2] + b:chunks[c][2] + b + n],
                                  ident[:, :])
                    last.then_inc(S["at_t"], 1)

                def values(c):
                    u = t_use["at", t, c]
                    need(pe, h, "t_evac", u + 1)
                    blocks = blocks_of(t, c)
                    for j, (b, slot, n) in enumerate(blocks):
                        last = mm(oar[:, 0, 0:VD], at[0:n, u % 2, b:b + P], vv[0:n, slot, :],
                                  start=(c == 0 and j == 0), stop=(c == len(chunks) - 1 and j == len(blocks) - 1))
                    return last

                transposes(0)
                for c in range(len(chunks)):
                    if t == SAMPLE - 1 and c == 1:
                        transpose_qk(h, SAMPLE)
                    if c + 1 < len(chunks):
                        transposes(c + 1)
                    last = values(c)
                    if t == SAMPLE - 1 and c == 1:
                        for m in range(2):
                            qk(h, SAMPLE, 0, m)
                last.then_inc(S["pv_done"], 1)

            def transpose_recurrence(h, t, first):
                if first and t + 1 < NT:
                    pe.wait_ge(S["x_lo"], t + 2)
                u = t_use["rec", t]
                need(pe, h, "t_evac", u - 1)
                need(pe, h, "nat_b", t + 1)
                tr(tb[:, u % 2, 0:P], nb[:, 0, :], ident[:, :])
                tr(tb[:, u % 2, P:2 * P], rc[:, 1, :], ident[:, :])
                tr(tb[:, u % 2, 2 * P:3 * P], nb[:, 1, :], ident[:, :]).then_inc(S["rect_t"], 1)

            def transpose_qk(h, t):
                u = t_use["q", t]
                need(pe, h, "t_evac", u - 1)
                need(pe, h, "qk_split", t + 1)
                for j in range(4):
                    last = tr(tb[:, u % 2, P * j:P * j + P], qn[:, j, :].bitcast(f32), ident[:, :])
                last.then_inc(S["q_t"], 1)
                u = t_use["k", t]
                need(pe, h, "t_evac", u - 1)
                if t == SAMPLE:
                    need(pe, h, "cache_split", 1)
                    for j in range(4):
                        last = tr(tb[:, u % 2, P * j:P * j + P], qn[:, (6, 4, 7, 5)[j], :].bitcast(f32), ident[:, :])
                else:
                    for j in range(2):
                        last = tr(tb[:, u % 2, P * j:P * j + P], qn[:, 4 + j, :].bitcast(f32), ident[:, :])
                last.then_inc(S["k_t"], 1)

            def qk_units(t):
                return [(c, m) for c in range(len(chunks_of(t))) for m in range(2)]

            def qk(h, t, c, m):
                if c == 0:
                    need(pe, h, "t_evac", t_use["k", t] + 1)
                k0, w, _ = chunks_of(t)[c]
                u = qk_use["qk", t, c, m]
                need(pe, h, "qk_free", u - 1)
                for part in range(2):
                    last = mm(qkb[:, u % 2, 0:w], q2[:, m, part, :], kp[:, m, k0:k0 + w],
                              start=(part == 0), stop=(part == 1))
                last.then_inc(S["qk_done"], 1)

            def head(h, first):
                for t in range(NT):
                    project(h, t, first)
                    if t > 0:
                        rec_output(h, t - 1)
                    if t > 0:
                        attend(h, t - 1, first)
                    if t < SAMPLE:
                        transpose_qk(h, t)
                rec_scores(h, SAMPLE)
                attend(h, SAMPLE, first)
                rec_output(h, SAMPLE)

            head(0, True)
            with pe.Fori(1, HEADS) as h:
                head(h, False)

            def epi_transposes(i, par):
                pe.wait_ge(S[f"mixin{par}"], 16 * i + 16)
                if not (isinstance(i, int) and i == 0 and par == 0):
                    pe.wait_ge(S["fo_lo"], 2 * i + par)
                for kt in range(KT):
                    last = tr(tb[:, kt // 4, P * (kt % 4):P * (kt % 4) + P],
                              heads_in[:, par, P * kt:P * kt + P], ident[:, :])
                last.then_inc(S["fo_t"], 1)

            def epi_project(i, par):
                pe.wait_ge(S["fo_lo"], 2 * i + (par + 1))
                past(pe, "fo_add", 2 * i + (par - 1))
                bank = (pab, qkb)[par]
                for kt in range(KT):
                    for part in range(2):
                        x = xr[:, par, part, kt, :]
                        for w in ((w_hi, w_lo) if part == 0 else (w_hi,)):
                            for b in range(2):
                                last = mm(bank[:, b, :], x, w[:, kt, 512 * b:512 * b + 512],
                                          start=(kt == 0 and part == 0 and w is w_hi),
                                          stop=(kt == KT - 1 and part == 1))
                last.then_inc(S["fo_mm"], 1)

            need(pe, HEADS - 1, "t_evac", T_USES)
            need(pe, HEADS - 1, "qk_free", QK_USES)
            epi_transposes(0, 0)
            need(pe, HEADS, "w_hi_ready", KT)
            need(pe, HEADS, "w_lo_vec", LO_PER["w_lo_vec"])
            need(pe, HEADS, "w_lo_pool", LO_PER["w_lo_pool"])
            with pe.Fori(0, PAIRS) as i:
                epi_transposes(i, 1)
                epi_project(i, 0)
                epi_transposes(i + 1, 0)
                epi_project(i, 1)
            epi_project(PAIRS, 0)

        @block.scalar
        def _(act):
            F = nc.scalar.activation
            prime(act, "scalar")
            nc.scalar.preload_act_table_set("natural_log_exp_and_others")

            def x_square(t):
                act.wait_ge(S[f"x_in{t % 2}"], 16 * (t // 2) + 16)
                if t > 0:
                    act.wait_ge(S["x_t"], t)
                F(x_norm, x_raw[t % 2], ACT.Square, accum_out=tsq[:, 0:1]).then_inc(S["x_sq"], 1)

            def x_high(t):
                act.wait_ge(S["x_t"], t + 1)
                if t >= XRING:
                    act.wait_ge(S[f"xs_out{t % XRING}"], 16 * (t // XRING))
                F(xr[:, t % XRING, 0], tb[:, :, :], ACT.Copy).then_inc(S["x_hi"], 1)

            def split_weights(h, pieces):
                first = isinstance(h, int) and h < 0
                for kt in pieces:
                    if not first:
                        if kt < KT - 1:
                            need(act, h, "w_freed", kt + 1)
                        else:
                            need(act, h, "proj_done", NT)
                    act.wait_ge(S[f"raw_in{kt}"], (h + 1) * 16 + 16)
                    F(w_hi[:, kt, :], raw_piece(h + 1, kt), ACT.Copy).then_inc(S["w_hi_ready"], 1)

            x_square(0)
            split_weights(-1, range(1))
            x_high(0)
            split_weights(-1, range(1, 3))
            x_square(1)
            split_weights(-1, range(3, KT))
            act.wait_ge(S["lam_dots"], 2)
            F(lam[:, 2:4], lam[:, 0:2], ACT.Exp).then_inc(S["setup_exp"], 1)
            act.wait_ge(S["lb_shifted"], 2)
            F(lbw[:, 2:4, :], lbw[:, 0:2, :], ACT.Exp).then_inc(S["setup_exp"], 1)
            x_high(1)

            def copy_decayed_keys(h, t):
                n = P if t < PT else DEC
                need(act, h, "kd_t", t + 1)
                F(kd[0:n, :], oar[0:n, 1, 256:384], ACT.Copy).then_inc(S["kd_evac"], 1)

            def attention_columns(h, t):
                need(act, h, "proj_done", t + 1)
                pa = pab[:, 0, :]
                q_out = qn[:, 0:4, :].rearrange("p (m a) (d e) -> p m a d e", m=2, d=2)[:, :, 0]
                q_in = pa[:, 0:P].rearrange("p (m e) -> p m e", m=2).unsqueeze(2).to_broadcast([P, 2, 2, HD])
                F(q_out, q_in, ACT.Copy)
                F(qn[:, 4:6, 0:HD], pa[:, P:2 * P].rearrange("p (m e) -> p m e", m=2), ACT.Copy)
                need(act, h, f"k_out{t % 2}", 16 * (t // 2))
                F(kn[:, t % 2, :], pa[:, P:2 * P], ACT.Copy)
                if t == 0:
                    need(act, h, "v_out", 0)
                F(vv[:, slot_of(t), :], pa[:, 2 * P:3 * P], ACT.Copy)
                F(zz[:, 0, :], pa[:, 3 * P:4 * P], ACT.Copy)
                F(ez[:, 0, :], pa[:, 3 * P:4 * P], ACT.Exp, scale=-1.0).then_inc(S["a_evac"], 1)

            def recurrence_columns(h, t):
                need(act, h, "proj_b", t + 1)
                pb = pab[:, 1, :]
                F(fb[:, :, :].rearrange("p g c -> p (g c)"), pb[:, 0:2 * P], ACT.Exp, scale=-1.0)
                F(vr[:, t % 2, :], pb[:, 2 * P:3 * P], ACT.Copy)
                need(act, h, "gates", t)
                F(zz[:, 1, :], pb[:, 3 * P:4 * P], ACT.Copy)
                F(ez[:, 1, :], pb[:, 3 * P:4 * P], ACT.Exp, scale=-1.0).then_inc(S["b_evac"], 1)

            def copy_weights(h, t, chunks):
                for c in chunks:
                    u = t_use["at", t, c]
                    w = P * len(blocks_of(t, c))
                    need(act, h, "at_t", at_index[t, c] + 1)
                    F(at[:, u % 2, 0:w], tb[:, u % 2, 0:w], ACT.Copy).then_inc(S["t_evac"], 1)

            def sum_squares(h, t):
                need(act, h, "rec_out", t + 1)
                need(act, h, "pv_done", t + 1)
                F(junk[:, 0:P], oar[:, 0, 0:P], ACT.Square, scale=rsum[:, 0:1], accum_out=ssq[:, 0:1])
                F(junk[:, P:2 * P], oar[:, 1, 0:P], ACT.Square, accum_out=ssq[:, 1:2]).then_inc(S["sumsq"], 1)

            def copy_recurrence(h, t):
                u = t_use["rec", t]
                need(act, h, "rect_t", t + 1)
                F(lf[:, :], tb[:, u % 2, P:2 * P], ACT.Ln, scale=lbh[:, 1:2], bias=lbh[:, 0:1])
                F(qt[:, :], tb[:, u % 2, 0:P], ACT.Copy)
                F(kt_[:, :], tb[:, u % 2, 2 * P:3 * P], ACT.Copy, scale=lbh[:, 1:2]).then_inc(S["t_evac"], 1)

            def copy_qk(h, t):
                u = t_use["q", t]
                need(act, h, "q_t", t + 1)
                F(q2[:, :, :, :].rearrange("p m a c -> p (m a c)"), tb[:, u % 2, :], ACT.Copy
                  ).then_inc(S["t_evac"], 1)
                u = t_use["k", t]
                need(act, h, "k_t", t + 1)
                first, w = (slot_of(t) * P, P) if t < PT else (CACHE_SLOT * P, 2 * P)
                F(kp[:, :, first:first + w], tb[:, u % 2, 0:2 * w].rearrange("p (m c) -> p m c", m=2), ACT.Copy
                  ).then_inc(S["t_evac"], 1)

            def softmax_exp(h, t):
                n = keys_of(t)[1]
                need(act, h, "neg_max", t + 1)
                for m in range(2):
                    last = F(scores[:, m, 0:n], scores[:, m, 0:n], ACT.Exp, bias=nmx[:, m:m + 1], scale=SCALE,
                             accum_out=sums[:, m:m + 1])
                last.then_inc(S["prob_ready"], 1)

            def decay_exp(h, t):
                need(act, h, "dist_ready", t + 1)
                if t > 0:
                    need(act, h, "k_decayed", t)
                    need(act, h, "q_decayed", t)
                F(xx[:, :, :], dd[:, :, :], ACT.Exp).then_inc(S["decay_ready"], 1)

            def head(h, first):
                for t in range(NT):
                    recurrence_columns(h, t)
                    if t > 0:
                        softmax_exp(h, t - 1)
                    if first and t + 2 < NT:
                        x_square(t + 2)
                    if t > 0:
                        copy_decayed_keys(h, t - 1)
                    if t == 0:
                        need(act, h, "head_set", 1)
                    copy_recurrence(h, t)
                    attention_columns(h, t)
                    if t < SAMPLE:
                        if t > 0:
                            copy_weights(h, t - 1, range(len(chunks_of(t - 1))))
                            sum_squares(h, t - 1)
                        copy_qk(h, t)
                        decay_exp(h, t)
                    if first and t + 2 < NT:
                        x_high(t + 2)
                assert len(chunks_of(SAMPLE - 1)) == 4 and KT == 8
                copy_weights(h, SAMPLE - 1, (0, 1))
                copy_qk(h, SAMPLE)
                split_weights(h, (0,))
                decay_exp(h, SAMPLE)
                copy_weights(h, SAMPLE - 1, (2,))
                split_weights(h, (1,))
                copy_weights(h, SAMPLE - 1, (3,))
                softmax_exp(h, SAMPLE)
                split_weights(h, (2,))
                sum_squares(h, SAMPLE - 1)
                split_weights(h, (3, 4))
                copy_decayed_keys(h, SAMPLE)
                split_weights(h, (5,))
                copy_weights(h, SAMPLE, (0,))
                split_weights(h, (6, 7))
                sum_squares(h, SAMPLE)

            head(0, True)
            with act.Fori(1, HEADS) as h:
                head(h, False)

            def epi_hi(i, par):
                act.wait_ge(S["fo_t"], 2 * i + (par + 1))
                past(act, "fo_mm", 2 * i + (par - 1))
                F(xr[:, par, 0], tb[:, :, :], ACT.Copy).then_inc(S["fo_hi"], 1)

            def epi_square(i, par):
                past(act, "fo_add", 2 * i + (par + 1))
                F(junk_rows[par], rows_in[:, par, :], ACT.Square,
                  accum_out=tsq[:, par:par + 1]).then_inc(S["fo_sq"], 1)

            epi_hi(0, 0)
            with act.Fori(0, PAIRS) as i:
                epi_hi(i, 1)
                epi_square(i, 0)
                epi_hi(i + 1, 0)
                epi_square(i, 1)
            epi_square(PAIRS, 0)

        @block.vector
        def _(dve):
            v = nc.vector
            tt, stt, ts = v.tensor_tensor, v.scalar_tensor_tensor, v.tensor_scalar
            prime(dve, "vector")
            setup = [0]

            def setup_link(ins):
                setup[0] += 1
                ins.then_inc(S["vec_setup"], 1)
                dve.wait_ge(S["vec_setup"], setup[0])

            def x_normalise(t):
                dve.wait_ge(S["x_rs"], t + 1)
                stt(x_norm, x_raw[t % 2], trs[:, 0:1], x_gain, ALU.mult, ALU.mult).then_inc(S["x_rows"], 1)

            def x_low(t):
                dve.wait_ge(S["x_hi"], t + 1)
                tt(xr[:, t % XRING, 1].rearrange("p k c -> p (k c)"), tb[:, :, :].rearrange("p b c -> p (b c)"),
                   xr[:, t % XRING, 0].rearrange("p k c -> p (k c)").bitcast(f32), ALU.subtract
                   ).then_inc(S["x_lo"], 1)

            def split_weights(h, pieces):
                for kt in pieces:
                    if kt not in LO_POOL:
                        need(dve, h + 1, "w_hi_ready", kt + 1)
                        tt(w_lo[:, kt, :], raw_piece(h + 1, kt), w_hi[:, kt, :].bitcast(f32), ALU.subtract
                           ).then_inc(S["w_lo_vec"], 1)

            v.memset(ones[:, :], 1.0)
            dve.wait_ge(S["gains_in"], 16)
            x_normalise(0)
            split_weights(-1, range(1))
            x_low(0)
            split_weights(-1, range(1, 3))
            x_normalise(1)
            split_weights(-1, range(3, KT))
            dve.wait_ge(S["const_in"], 80)
            for j in range(2):
                v.tensor_tensor_reduce(out=nb[:, j, 0:HD], in0=lamv[:, 2 * j, :], in1=lamv[:, 2 * j + 1, :], scale=1.0,
                                       scalar=0.0, op0=ALU.mult, op1=ALU.add, accum_out=lam[:, j:j + 1]
                                       ).then_inc(S["lam_dots"], 1)
            setup_link(tt(lb[:, :], lbr[:, 0, :], lbr[:, 1, :], ALU.max))
            for r in range(2):
                tt(lbw[:, r, :], lbr[:, r, :], lb[:, :], ALU.subtract).then_inc(S["lb_shifted"], 1)
            dve.wait_ge(S["setup_exp"], 2)
            setup_link(tt(lam[:, 4:5], lam[:, 3:4], lam[:, 2:3], ALU.subtract))
            setup_link(v.tensor_scalar_add(lam[:, 5:6], lam[:, 4:5], -LAM_INIT))
            setup_link(tt(lb[:, :], lbw[:, 2, :], lbw[:, 3, :], ALU.add))
            setup_link(v.reciprocal(oml[:, :], lb[:, :]))
            setup_link(tt(lb[:, :], lbw[:, 2, :], oml[:, :], ALU.mult))
            setup_link(tt(oml[:, :], lbw[:, 3, :], oml[:, :], ALU.mult))
            setup_link(ts(gains2[:, 0, :], gains2[:, 0, :], 1.0 - LAM_INIT, None, ALU.mult))
            chain = [0]

            def link(h, ins):
                chain[0] += 1
                ins.then_inc(S["vec_chain"], 1)
                need(dve, h, "vec_chain", chain[0])

            def make_bias():
                dve.wait_ge(S["w_lo_pool"], len(LO_POOL))
                for part in range(2):
                    dve.wait_ge(S["table_ready"], part + 1)
                    last = v.tensor_copy(bias[:, 1024 * part:1024 * part + 1024], tables[part])
                setup_link(last)
                setup_link(stt(bias[:, :], bias[:, :], -1.0, bias[:, :], ALU.mult, ALU.min))
                setup_link(v.memset(bias[0:CHUNK, SEQ - CHUNK:SEQ], MASKED))

            def head_start(h):
                if not (isinstance(h, int) and h == 0):
                    ts(bias[:, :], bias[:, :], 0.25, None, ALU.mult)
                need(dve, h, "h_out", 0)
                v.memset(state[:, :], 0.0)
                v.tensor_copy(lbh[:, 0:1], lb[:, bass.ds(h, 1)])
                v.tensor_copy(lbh[:, 1:2], oml[:, bass.ds(h, 1)]).then_inc(S["head_set"], 1)

            def sum_scores(h, t):
                need(dve, h, "kscore_done", t + 1)
                for part, (a, b) in enumerate(((0, 4), (4, NS - 1))):
                    u = qk_use["rec", t, part]
                    tt(masked[:, a:b, :], qkb[:, u % 2, 0:P * (b - a)].rearrange("p (l c) -> p l c", c=P),
                       causal[:, a:b, :], ALU.mult).then_inc(S["qk_free"], 1)
                need(dve, h, "qk_free", u + 1)
                v.tensor_reduce(st[:, :], masked[:, :, :].rearrange("p l c -> p c l"), AX.X, ALU.add
                                ).then_inc(S["rec_acc"], 1)

            def attention_columns(h, t):
                need(dve, h, "a_evac", t + 1)
                pa = pab[:, 0, :]
                q_blocks = qn[:, 0:4, :].rearrange("p (m a) (d e) -> p m a d e", m=2, d=2)
                q_in = pa[:, 0:P].rearrange("p (m e) -> p m e", m=2).unsqueeze(2).to_broadcast([P, 2, 2, HD])
                tt(q_blocks[:, :, 1], q_in, q_blocks[:, :, 0].bitcast(f32), ALU.subtract)
                tt(qn[:, 4:6, HD:P], pa[:, P:2 * P].rearrange("p (m e) -> p m e", m=2),
                   qn[:, 4:6, 0:HD].bitcast(f32), ALU.subtract).then_inc(S["qk_split"], 1)
                if t == SAMPLE:
                    need(dve, h, "cache_in", 48)
                    k_in = kc[:, :].rearrange("p (m e) -> p m e", m=2)
                    link(h, v.tensor_copy(qn[:, 6:8, 0:HD], k_in))
                    tt(qn[:, 6:8, HD:P], k_in, qn[:, 6:8, 0:HD].bitcast(f32), ALU.subtract
                       ).then_inc(S["cache_split"], 1)

            def recurrence_columns(h, t):
                need(dve, h, "b_evac", t + 1)
                ts(rc[:, 1, :], fb[:, 1, :], FMAX, 1.0, ALU.min, ALU.add)
                link(h, v.tensor_scalar_add(rc[:, 0, :], fb[:, 0, :], 1.0))
                link(h, v.reciprocal(rc[:, :, :], rc[:, :, :]))
                tt(nb[:, 0, :], pab[:, 1, 0:P], rc[:, 0, :], ALU.mult).then_inc(S["pb_free"], 1)
                stt(nb[:, 1, :], fb[:, 1, :], FMAX, rc[:, 1, :], ALU.min, ALU.mult).then_inc(S["nat_b"], 1)

            def gate_sigmoids(h, t):
                link(h, v.tensor_scalar_add(ez[:, :, :], ez[:, :, :], 1.0))
                v.reciprocal(ez[:, :, :], ez[:, :, :]).then_inc(S["z_ready"], 1)

            def finish(h, t):
                need(dve, h, "rs_ready", t + 1)
                need(dve, h, "gates", t + 1)
                need(dve, h, f"mix_out{t % 2}", 16 * (t // 2))
                stt(mx[:, t % 2, 0, :], oar[:, 0, 0:P], rsa[:, 0:1], gate[:, t % 2, 0, :], ALU.mult, ALU.mult)
                s = state if t < PT else state_s
                stt(s[:, :], s[:, :], total[:, t % 2:t % 2 + 1], oar[:, 1, P:2 * P], ALU.mult, ALU.add)
                stt(mx[:, t % 2, 1, :], oar[:, 1, 0:P], rs[:, 1:2], gate[:, t % 2, 1, :], ALU.mult, ALU.mult
                    ).then_inc(S["fin_done"], 1)

            def accumulate_decay(h, t):
                need(dve, h, "t_evac", t_use["rec", t] + 1)
                v.tensor_tensor_scan(dd[:, NX - 1, :], ones[:, :], lf[:, :], 0.0, ALU.mult, ALU.add
                                     ).then_inc(S["cum_ready"], 1)

            def biased_scores(h, t):
                chunks = chunks_of(t)
                zero = SEQ - P - P * (t if t < PT else 1)
                for c, (_, w, off) in enumerate(chunks):
                    for m in range(2):
                        u = qk_use["qk", t, c, m]
                        if t == SAMPLE and m == 0:
                            need(dve, h, "at_t", at_index[t - 1, 0] + 1)
                        need(dve, h, "qk_done", qk_index[t, c, m] + 1)
                        if c > 0:
                            need(dve, h, "qk_free", u - 1)
                        apart(dve)
                        v.tensor_tensor_reduce(
                            out=scores[:, m, off:off + w], in0=qkb[:, u % 2, 0:w],
                            in1=bias[:, zero + off:zero + off + w], scale=1.0,
                            scalar=(mxs[:, m, c - 1:c] if c else -3e38), op0=ALU.add, op1=ALU.max,
                            accum_out=mxs[:, m, c:c + 1]).then_inc(S["qk_free"], 1)
                    if c == 0 and len(chunks) > 1 and t > 0:
                        finish(h, t - 1)
                    if c == 1:
                        apply_decay(h, t)
                need(dve, h, "qk_free", u + 1)
                ts(nmx[:, :], mxs[:, :, len(chunks) - 1], -SCALE, None, ALU.mult).then_inc(S["neg_max"], 1)
                if len(chunks) == 1 and t < SAMPLE:
                    if t > 0:
                        finish(h, t - 1)
                    apply_decay(h, t)

            def combine(h, t):
                need(dve, h, "prob_ready", t + 1)
                link(h, v.reciprocal(rsum[:, :], sums[:, :]))
                link(h, stt(cneg[:, :], sums[:, 0:1], rsum[:, 1:2], lam[:, 5:6], ALU.mult, ALU.mult))
                for _, w, off in chunks_of(t):
                    stt(scores[:, 0, off:off + w], scores[:, 1, off:off + w], cneg[:, 0:1], scores[:, 0, off:off + w],
                        ALU.mult, ALU.add).then_inc(S["combined"], 1)

            def apply_decay(h, t):
                at_last = P - 1 if t < PT else DEC - 1
                need(dve, h, "decay_ready", t + 1)
                v.tensor_copy(total[:, t % 2:t % 2 + 1], xx[:, NX - 1, at_last:at_last + 1])
                tt(kl[:, :, :], kt_[:, :].unsqueeze(1).to_broadcast([P, NS, P]), xx[:, 0:NS, :], ALU.mult
                   ).then_inc(S["k_decayed"], 1)

            def head(h, first):
                chain[0] = 0
                head_start(h)
                for t in range(NT):
                    recurrence_columns(h, t)
                    if t > 0:
                        sum_scores(h, t - 1)
                        combine(h, t - 1)
                    if first and t == 0:
                        x_low(1)
                    accumulate_decay(h, t)
                    attention_columns(h, t)
                    if first and t + 2 < NT:
                        x_normalise(t + 2)
                    gate_sigmoids(h, t)
                    if first and t == 0:
                        make_bias()
                    biased_scores(h, t)
                    if first and t + 2 < NT:
                        x_low(t + 2)
                apply_decay(h, SAMPLE)
                split_weights(h, range(4))
                finish(h, SAMPLE - 1)
                combine(h, SAMPLE)
                sum_scores(h, SAMPLE)
                split_weights(h, range(4, KT))
                finish(h, SAMPLE)

            head(0, True)
            with dve.Fori(1, HEADS) as h:
                head(h, False)
            assert chain[0] == PER["vec_chain"], chain[0]

            def epi_lo(i, par):
                dve.wait_ge(S["fo_hi"], 2 * i + (par + 1))
                tt(xr[:, par, 1].rearrange("p k c -> p (k c)"), tb[:, :, :].rearrange("p b c -> p (b c)"),
                   xr[:, par, 0].rearrange("p k c -> p (k c)").bitcast(f32), ALU.subtract
                   ).then_inc(S["fo_lo"], 1)

            def epi_add(i, par):
                dve.wait_ge(S[f"rowsin{par}"], 16 * i + 16)
                apart(dve)
                dve.wait_ge(S["fo_mm"], 2 * i + (par + 1 + PRIME["fo_mm"]))
                rows = rows_in[:, par, :]
                tt(rows, (pab, qkb)[par][:, :, :].rearrange("p b c -> p (b c)"), rows, ALU.add
                   ).then_inc(S["fo_add"], 1)

            def epi_normalise(i, par):
                dve.wait_ge(S["fo_rs"], 2 * i + (par + 1))
                past(dve, f"y_out{par}", 16 * i)
                stt(xn[:, par, :], rows_in[:, par, :], trs[:, par:par + 1], gains[:, :],
                    ALU.mult, ALU.mult).then_inc(S["fo_y"], 1)

            epi_lo(0, 0)
            dve.wait_ge(S["gains_in"], 32)
            with dve.Fori(0, PAIRS) as i:
                epi_lo(i, 1)
                epi_add(i, 0)
                epi_normalise(i, 0)
                epi_lo(i + 1, 0)
                epi_add(i, 1)
                epi_normalise(i, 1)
            epi_add(PAIRS, 0)
            epi_normalise(PAIRS, 0)

        @block.gpsimd
        def _(pool):
            g = nc.gpsimd
            prime(pool, "gpsimd")
            setup = [0]

            def setup_link(ins):
                setup[0] += 1
                ins.then_inc(S["pool_setup"], 1)
                pool.wait_ge(S["pool_setup"], setup[0])

            g.memset(half[:, :], -0.5)
            g.memset(ident[:, :], 0.0)
            setup_link(g.memset(causal[:, :, :], 1.0))
            g.affine_select(out=ident[:, :], in_=ident[:, :], compare_op=ALU.not_equal, fill=1.0, base=0,
                            pattern=[[-1, P]], channel_multiplier=1).then_inc(S["masks_ready"], 1)
            def row_scale(ready, signal, n, par):
                pool.wait_ge(S[ready], n)
                apart(pool)
                g.tensor_scalar(tms[:, par:par + 1], tsq[:, par:par + 1], 1.0 / D_MODEL, EPS, ALU.mult, ALU.add
                                ).then_inc(S[signal + "_mean"], 1)
                pool.wait_ge(S[signal + "_mean"], n)
                g.tensor_tensor(trs[:, par:par + 1], tms[:, par:par + 1], half[:, 0:1], ALU.pow
                                ).then_inc(S[signal], 1)

            def split_weights(h, pieces):
                for kt in pieces:
                    need(pool, h + 1, "w_hi_ready", kt + 1)
                    g.tensor_tensor(w_lo[:, kt, :], raw_piece(h + 1, kt), w_hi[:, kt, :].bitcast(f32), ALU.subtract
                                    ).then_inc(S["w_lo_pool"], 1)

            row_scale("x_sq", "x_rs", 1, 0)
            row_scale("x_sq", "x_rs", 2, 0)
            split_weights(-1, LO_POOL)
            name, n = lo_of(3)
            pool.wait_ge(S[name], n)
            for part in range(2):
                g.iota(tables[part], pattern=[[-2, 1024]], base=2 * (SEQ - P - 1024 * part),
                       channel_multiplier=2).then_inc(S["table_ready"], 1)

            def keep(out, pattern, base, step):
                return g.affine_select(out=out, in_=out, compare_op=ALU.is_ge, fill=0.0, base=base,
                                       pattern=pattern, channel_multiplier=step)

            for j, size in enumerate((BASE,) + tuple(2 * s for s in HALVES)):
                nblk = P // size
                out = causal[:, j, :].rearrange("p (b r) -> p b r", b=nblk)
                setup_link(keep(out, [[-size, nblk], [0, size]], 0, 1))
                if j == 0:
                    setup_link(keep(out, [[size, nblk], [1, size]], 0, -1))
                else:
                    setup_link(keep(out, [[size, nblk], [0, size]], size // 2 - 1, -1))
                    setup_link(keep(out, [[0, nblk], [1, size]], -(size // 2), 0))

            chain = [0]

            def link(h, ins):
                chain[0] += 1
                ins.then_inc(S["pool_chain"], 1)
                need(pool, h, "pool_chain", chain[0])

            def gates(h, t):
                need(pool, h, "z_ready", t + 1)
                link(h, g.tensor_tensor(zz[:, :, :], zz[:, :, :], ez[:, :, :], ALU.mult))
                g.tensor_tensor(gate[:, t % 2, :, :], zz[:, :, :], gains2[:, :, :], ALU.mult).then_inc(S["gates"], 1)

            def apply_decay(h, t):
                need(pool, h, "decay_ready", t + 1)
                g.tensor_tensor(ql[:, :, :], qt[:, :].unsqueeze(1).to_broadcast([P, NS, P]), xx[:, NX - NS:NX, :],
                                ALU.mult).then_inc(S["q_decayed"], 1)

            def head_scales(h, t):
                need(pool, h, "sumsq", t + 1)
                apart(pool)
                link(h, g.tensor_scalar(ms[:, :], ssq[:, :], 1.0 / VD, EPS, ALU.mult, ALU.add))
                link(h, g.tensor_tensor(rs[:, :], ms[:, :], half[:, :], ALU.pow))
                g.tensor_tensor(rsa[:, :], rs[:, 0:1], rsum[:, 0:1], ALU.mult).then_inc(S["rs_ready"], 1)

            def exponents(h, t):
                n = P if t < PT else DEC
                need(pool, h, "cum_ready", t + 1)
                cum = dd[:, NX - 1, :]
                sub = ALU.subtract
                for j, s in enumerate(HALVES):
                    c = cum.rearrange("p (b a r) -> p b a r", a=2, r=s)
                    o = dd[:, 2 + j, :].rearrange("p (b a r) -> p b a r", a=2, r=s)
                    ref = c[:, :, 0, s - 1:s].to_broadcast([P, P // (2 * s), s])
                    g.tensor_tensor(o[:, :, 0, :], ref, c[:, :, 0, :], sub)
                    g.tensor_tensor(o[:, :, 1, :], c[:, :, 1, :], ref, sub)
                c = cum.rearrange("p (b r) -> p b r", r=BASE)
                ref = c[:, :, 1:2].to_broadcast([P, P // BASE, BASE])
                g.tensor_tensor(dd[:, 1, :].rearrange("p (b r) -> p b r", r=BASE), ref, c, sub)
                g.tensor_tensor(dd[:, NX - 2, :].rearrange("p (b r) -> p b r", r=BASE), c, ref, sub)
                g.tensor_tensor(dd[:, 0, 0:n], cum[:, n - 1:n].to_broadcast([P, n]), cum[:, 0:n], sub
                                ).then_inc(S["dist_ready"], 1)

            def head(h, first):
                chain[0] = 0
                for t in range(NT):
                    if first and t + 2 < NT:
                        row_scale("x_sq", "x_rs", t + 3, 0)
                    exponents(h, t)
                    if t == SAMPLE:
                        apply_decay(h, t)
                    if t > 0:
                        head_scales(h, t - 1)
                    if t < SAMPLE:
                        apply_decay(h, t)
                    gates(h, t)
                split_weights(h, LO_POOL)
                head_scales(h, SAMPLE)

            head(0, True)
            with pool.Fori(1, HEADS) as h:
                head(h, False)
            assert chain[0] == PER["pool_chain"]

            with pool.Fori(0, PAIRS) as i:
                for par in range(2):
                    row_scale("fo_sq", "fo_rs", 2 * i + (par + 1), par)
            row_scale("fo_sq", "fo_rs", NT, 0)


_INS = ["x_prompt", "x_sample", "cache_k", "cache_v", "state_h", "norm_g", "w_in", "lambda_qk", "subln_g", "rec_lb",
        "rec_norm_g", "w_out", "final_g"]
_OUTS = [(1, SEQ, D_MODEL), (1, DEC, D_MODEL), (1, 1, SEQ, HEADS, 2 * HD), (1, 1, SEQ, HEADS, VD),
         (1, 1, HEADS, VD, VD), (1, 1, DEC, HEADS, 2 * HD), (1, 1, DEC, HEADS, VD), (1, 1, HEADS, VD, VD)]


def kernel(**inputs):
    import concourse.bacc as bacc
    from concourse.bass_utils import run_bass_kernel_spmd

    nc = bacc.Bacc("TRN2", target_bir_lowering=False, num_devices=1)
    arrays, args = {}, []
    for name in _INS:
        a = np.ascontiguousarray(inputs[name])
        arrays[f"in_{name}"] = a
        args.append(nc.dram_tensor(f"in_{name}", a.shape, mybir.dt.from_np(a.dtype), kind="ExternalInput").ap())
    for i, shape in enumerate(_OUTS):
        args.append(nc.dram_tensor(f"out_{i}", shape, mybir.dt.float32, kind="ExternalOutput").ap())
    build(nc, *args)
    r = run_bass_kernel_spmd(nc, [arrays], core_ids=[0])
    return tuple(r.results[0][f"out_{i}"] for i in range(len(_OUTS)))
```
